# Optimizing a Trainium2 kernel written in Bass

```python
import math
import jax, jax.numpy as jnp
from jax import lax
import numpy as np

D_MODEL = 1024
BATCH = 1
SEQ = 512
DEPTH = 2

CHUNK = 64
N_MIXERS = 4
GROUP_WIDTH = D_MODEL // N_MIXERS
MIX_WIDTH = N_MIXERS * GROUP_WIDTH

GM_HEADS = 4
GM_HEAD_DIM = GROUP_WIDTH // GM_HEADS
GM_BLOCK = 128
MLA_HEADS = 4
MLA_NOPE_DIM = 64
MLA_ROPE_DIM = 32
MLA_QK_DIM = MLA_NOPE_DIM + MLA_ROPE_DIM
MLA_V_DIM = GROUP_WIDTH // MLA_HEADS
MLA_Q_RANK = 192
MLA_KV_RANK = 128
ROPE_THETA = 10000.0
ATTN_BLOCK = 128
S5_GROUP = 16
S5_GROUPS = GROUP_WIDTH // S5_GROUP
S5_STATE = 64
S5_DT_MIN = 1e-3
S5_DT_MAX = 1e-1
HG_HEADS = 4
HG_DK = GROUP_WIDTH // HG_HEADS
HG_DV = GROUP_WIDTH // HG_HEADS
D_FF = 2816
CONV_W = 3
DN_ALPHA = (2 * DEPTH) ** 0.25
DN_BETA = (8 * DEPTH) ** -0.25
ADA_SCALE = 0.25

IN_SIZES = (GROUP_WIDTH, GROUP_WIDTH, MLA_Q_RANK, MLA_KV_RANK, MLA_ROPE_DIM,
            GROUP_WIDTH, GROUP_WIDTH, GROUP_WIDTH, GROUP_WIDTH, GROUP_WIDTH)
IN_COLS = sum(IN_SIZES)
IN_SPLITS = tuple(sum(IN_SIZES[:i + 1]) for i in range(len(IN_SIZES) - 1))

kernel_name = "hybrid_streaming_encoder_block"

def layer_norm(x, g, b, eps=1e-5):
    xf = x.astype(jnp.float32)
    mu = jnp.mean(xf, -1, keepdims=True)
    var = jnp.mean(jnp.square(xf - mu), -1, keepdims=True)
    return ((xf - mu) * lax.rsqrt(var + eps)).astype(x.dtype) * g + b

def rms_norm(x, g, eps=1e-6):
    xf = x.astype(jnp.float32)
    return (xf * lax.rsqrt(jnp.mean(xf * xf, -1, keepdims=True) + eps)).astype(x.dtype) * g

def spatial_gating(u, v, ln_g, ln_b, w_s, b_s):
    bsz, L, _ = v.shape
    nb = L // GM_BLOCK
    vn = layer_norm(v, ln_g, ln_b).reshape(bsz, nb, GM_BLOCK, GM_HEADS, GM_HEAD_DIM)
    ck = jnp.arange(GM_BLOCK) // CHUNK
    mask = ck[None, :] <= ck[:, None]
    w = jnp.where(mask[None], w_s, 0).astype(v.dtype)
    z = jnp.einsum('hij,bnjhd->bnihd', w, vn) + b_s.T[:, :, None]
    return u * z.reshape(bsz, L, GROUP_WIDTH)

def rope_tables(L):
    inv = 1.0 / (ROPE_THETA ** (jnp.arange(0, MLA_ROPE_DIM, 2, dtype=jnp.float32) / MLA_ROPE_DIM))
    ang = jnp.arange(L, dtype=jnp.float32)[:, None] * inv[None, :]
    return jnp.cos(ang), jnp.sin(ang)

def apply_rope(x, cos, sin):
    x1, x2 = jnp.split(x.astype(jnp.float32), 2, axis=-1)
    cc, ss = cos[:, None, :], sin[:, None, :]
    return jnp.concatenate([x1 * cc - x2 * ss, x1 * ss + x2 * cc], -1).astype(x.dtype)

def chunk_causal_attention(q, k, v):
    bsz, L, H, dq = q.shape
    nb = L // ATTN_BLOCK
    qb = jnp.moveaxis(q.reshape(bsz, nb, ATTN_BLOCK, H, dq), 1, 0)
    kchunk = jnp.arange(L) // CHUNK

    def one_block(args):
        qi, bi = args
        qchunk = (bi * ATTN_BLOCK + jnp.arange(ATTN_BLOCK)) // CHUNK
        s = jnp.einsum('bqhd,bkhd->bhqk', qi, k, preferred_element_type=jnp.float32)
        s = jnp.where(kchunk[None, :] <= qchunk[:, None], s, -jnp.inf)
        p = jax.nn.softmax(s, axis=-1).astype(v.dtype)
        return jnp.einsum('bhqk,bkhd->bqhd', p, v)

    out = lax.map(one_block, (qb, jnp.arange(nb)))
    return jnp.moveaxis(out, 0, 1).reshape(bsz, L, H, v.shape[-1])

def mla(cq, ckv, kr, q_norm, kv_norm, w_uq, w_ukv):
    bsz, L, _ = cq.shape
    q = (rms_norm(cq, q_norm) @ w_uq).reshape(bsz, L, MLA_HEADS, MLA_QK_DIM)
    kv = (rms_norm(ckv, kv_norm) @ w_ukv).reshape(bsz, L, MLA_HEADS, MLA_NOPE_DIM + MLA_V_DIM)
    cos, sin = rope_tables(L)
    q_rope = apply_rope(q[..., MLA_NOPE_DIM:], cos, sin)
    k_rope = apply_rope(kr[:, :, None, :], cos, sin)
    k = jnp.concatenate([kv[..., :MLA_NOPE_DIM],
                         jnp.broadcast_to(k_rope, (bsz, L, MLA_HEADS, MLA_ROPE_DIM))], -1)
    v = kv[..., MLA_NOPE_DIM:]
    qf = jnp.concatenate([q[..., :MLA_NOPE_DIM], q_rope], -1) * (MLA_QK_DIM ** -0.5)
    return chunk_causal_attention(qf, k, v).reshape(bsz, L, GROUP_WIDTH)

def s5(u, a_re, a_im, b_re, b_im, c_re, c_im, d, log_step, w_glu, b_glu):
    f32 = jnp.float32
    bsz, L, _ = u.shape
    uf = u.astype(f32).reshape(bsz, L, S5_GROUPS, S5_GROUP)
    ar, ai = a_re.astype(f32), a_im.astype(f32)
    dt = jnp.exp(log_step.astype(f32))[:, None]
    mag = jnp.exp(dt * ar)
    abar_re, abar_im = mag * jnp.cos(dt * ai), mag * jnp.sin(dt * ai)
    den = ar * ar + ai * ai
    nr, ni = abar_re - 1.0, abar_im
    zoh_re = (nr * ar + ni * ai) / den
    zoh_im = (ni * ar - nr * ai) / den
    br, bi = b_re.astype(f32), b_im.astype(f32)
    bbar_re = zoh_re[..., None] * br - zoh_im[..., None] * bi
    bbar_im = zoh_re[..., None] * bi + zoh_im[..., None] * br
    bu_re = jnp.einsum('blgn,gpn->blgp', uf, bbar_re)
    bu_im = jnp.einsum('blgn,gpn->blgp', uf, bbar_im)
    a_r = jnp.broadcast_to(abar_re, bu_re.shape)
    a_i = jnp.broadcast_to(abar_im, bu_im.shape)

    def combine(e1, e2):
        a1r, a1i, b1r, b1i = e1
        a2r, a2i, b2r, b2i = e2
        return (a2r * a1r - a2i * a1i, a2r * a1i + a2i * a1r,
                a2r * b1r - a2i * b1i + b2r, a2r * b1i + a2i * b1r + b2i)

    _, _, hr, hi = lax.associative_scan(combine, (a_r, a_i, bu_re, bu_im), axis=1)
    y = (jnp.einsum('blgp,gnp->blgn', hr, c_re.astype(f32))
         - jnp.einsum('blgp,gnp->blgn', hi, c_im.astype(f32)))
    y = y + d.astype(f32).reshape(S5_GROUPS, S5_GROUP) * uf
    z = jax.nn.gelu(y.reshape(bsz, L, GROUP_WIDTH).astype(u.dtype))
    return z * jax.nn.sigmoid(z @ w_glu + b_glu)

def hgrn2(q, f_logit, i, g, lb, gn_g):
    f32 = jnp.float32
    bsz, L, _ = q.shape
    nc = L // CHUNK
    f = lb + (1.0 - lb) * jax.nn.sigmoid(f_logit.astype(f32))
    logf = jnp.log(f)
    shp = lambda t, dd: t.reshape(bsz, nc, CHUNK, HG_HEADS, dd)
    qc = shp(q.astype(f32), HG_DK)
    kc = shp(1.0 - f, HG_DK)
    vc = shp(i.astype(f32), HG_DV)
    b = jnp.cumsum(shp(logf, HG_DK), axis=2)
    b_last = b[:, :, -1]
    causal = jnp.tril(jnp.ones((CHUNK, CHUNK), dtype=bool))

    def intra(args):
        qn, kn, vn, bn = args
        rel = jnp.where(causal[None, :, :, None, None], bn[:, :, None] - bn[:, None, :], -jnp.inf)
        att = jnp.einsum('bthk,bshk,btshk->bhts', qn, kn, jnp.exp(rel))
        return jnp.einsum('bhts,bshv->bthv', att, vn)

    mv = lambda t: jnp.moveaxis(t, 1, 0)
    o_intra = jnp.moveaxis(lax.map(intra, (mv(qc), mv(kc), mv(vc), mv(b))), 0, 1)
    u_chunk = jnp.einsum('bnshk,bnshv->bnhkv', kc * jnp.exp(b_last[:, :, None] - b), vc)
    decay_chunk = jnp.exp(b_last)

    def step(S, inp):
        dch, uch = inp
        return dch[..., None] * S + uch, S

    S0 = jnp.zeros((bsz, HG_HEADS, HG_DK, HG_DV), f32)
    _, S_in = lax.scan(step, S0, (mv(decay_chunk), mv(u_chunk)))
    S_in = jnp.moveaxis(S_in, 0, 1)
    o_inter = jnp.einsum('bnthk,bnhkv->bnthv', qc * jnp.exp(b), S_in)
    o = rms_norm(o_intra + o_inter, gn_g.astype(f32).reshape(HG_HEADS, HG_DV))
    o = o.reshape(bsz, L, GROUP_WIDTH).astype(q.dtype)
    return o * jax.nn.sigmoid(g)

def conv_ffn(h, w_up, conv_w, conv_b, w_down):
    a = h @ w_up
    a = lax.conv_general_dilated(a, conv_w[:, None, :].astype(a.dtype), window_strides=(1,),
                                 padding=[(CONV_W - 1, 0)],
                                 dimension_numbers=('NWC', 'WIO', 'NWC'),
                                 feature_group_count=a.shape[-1]) + conv_b
    val, gate = jnp.split(a, 2, axis=-1)
    return (val * jax.nn.silu(gate)) @ w_down

def setup_inputs(seed: int = 0) -> dict:
    key = jax.random.key(seed)
    ks = iter(jax.random.split(key, 48))
    L = DEPTH
    D = D_MODEL
    GW = GROUP_WIDTH

    def nrm(shape, scale):
        return jax.random.normal(next(ks), shape, jnp.float32) * scale

    def gain(shape):
        return 1.0 + nrm(shape, 0.02)

    x = nrm((BATCH, SEQ, D), 1.0)
    c = nrm((BATCH, D), 1.0)
    ln_in_g = gain((D,))
    ln_in_b = nrm((D,), 0.02)
    hg_lb_logits = nrm((L, GW), 1.0)
    w_ada = nrm((L, D, 6 * D), ADA_SCALE * D ** -0.5)
    b_ada = nrm((L, 6 * D), 0.02)
    w_in = nrm((L, D, IN_COLS), D ** -0.5)
    gm_ln_g = gain((L, GW))
    gm_ln_b = nrm((L, GW), 0.02)
    gm_ws = nrm((L, GM_HEADS, GM_BLOCK, GM_BLOCK), GM_BLOCK ** -0.5)
    gm_bs = 1.0 + nrm((L, GM_HEADS, GM_BLOCK), 0.02)
    mla_q_norm = gain((L, MLA_Q_RANK))
    mla_kv_norm = gain((L, MLA_KV_RANK))
    mla_w_uq = nrm((L, MLA_Q_RANK, MLA_HEADS * MLA_QK_DIM), MLA_Q_RANK ** -0.5)
    mla_w_ukv = nrm((L, MLA_KV_RANK, MLA_HEADS * (MLA_NOPE_DIM + MLA_V_DIM)), MLA_KV_RANK ** -0.5)
    s5_a_re = -0.5 + nrm((L, S5_GROUPS, S5_STATE), 0.01)
    s5_a_im = math.pi * jnp.arange(S5_STATE, dtype=jnp.float32) + nrm((L, S5_GROUPS, S5_STATE), 0.01)
    s5_b_re = nrm((L, S5_GROUPS, S5_STATE, S5_GROUP), (2 * S5_GROUP) ** -0.5)
    s5_b_im = nrm((L, S5_GROUPS, S5_STATE, S5_GROUP), (2 * S5_GROUP) ** -0.5)
    s5_c_re = nrm((L, S5_GROUPS, S5_GROUP, S5_STATE), (2 * S5_STATE) ** -0.5)
    s5_c_im = nrm((L, S5_GROUPS, S5_GROUP, S5_STATE), (2 * S5_STATE) ** -0.5)
    s5_d = nrm((L, GW), 1.0)
    s5_log_step = jax.random.uniform(next(ks), (L, S5_GROUPS), jnp.float32,
                                     minval=math.log(S5_DT_MIN), maxval=math.log(S5_DT_MAX))
    s5_w_glu = nrm((L, GW, GW), GW ** -0.5)
    s5_b_glu = nrm((L, GW), 0.02)
    hg_norm_g = gain((L, GW))
    merge_g = gain((L, MIX_WIDTH))
    w_out = nrm((L, MIX_WIDTH, D), MIX_WIDTH ** -0.5 * DN_BETA)
    ln1_g = gain((L, D))
    ln1_b = nrm((L, D), 0.02)
    w_up = nrm((L, D, 2 * D_FF), D ** -0.5)
    conv_w = nrm((L, CONV_W, 2 * D_FF), CONV_W ** -0.5)
    conv_b = nrm((L, 2 * D_FF), 0.02)
    w_down = nrm((L, D_FF, D), D_FF ** -0.5 * DN_BETA)
    ln2_g = gain((L, D))
    ln2_b = nrm((L, D), 0.02)
    return {"x": x, "c": c, "ln_in_g": ln_in_g, "ln_in_b": ln_in_b, "hg_lb_logits": hg_lb_logits,
            "w_ada": w_ada, "b_ada": b_ada, "w_in": w_in, "gm_ln_g": gm_ln_g, "gm_ln_b": gm_ln_b,
            "gm_ws": gm_ws, "gm_bs": gm_bs, "mla_q_norm": mla_q_norm, "mla_kv_norm": mla_kv_norm,
            "mla_w_uq": mla_w_uq, "mla_w_ukv": mla_w_ukv, "s5_a_re": s5_a_re, "s5_a_im": s5_a_im,
            "s5_b_re": s5_b_re, "s5_b_im": s5_b_im, "s5_c_re": s5_c_re, "s5_c_im": s5_c_im,
            "s5_d": s5_d, "s5_log_step": s5_log_step, "s5_w_glu": s5_w_glu, "s5_b_glu": s5_b_glu,
            "hg_norm_g": hg_norm_g, "merge_g": merge_g, "w_out": w_out, "ln1_g": ln1_g,
            "ln1_b": ln1_b, "w_up": w_up, "conv_w": conv_w, "conv_b": conv_b, "w_down": w_down,
            "ln2_g": ln2_g, "ln2_b": ln2_b}

def reference(x, c, ln_in_g, ln_in_b, hg_lb_logits, w_ada, b_ada, w_in, gm_ln_g, gm_ln_b,
              gm_ws, gm_bs, mla_q_norm, mla_kv_norm, mla_w_uq, mla_w_ukv, s5_a_re, s5_a_im,
              s5_b_re, s5_b_im, s5_c_re, s5_c_im, s5_d, s5_log_step, s5_w_glu, s5_b_glu,
              hg_norm_g, merge_g, w_out, ln1_g, ln1_b, w_up, conv_w, conv_b, w_down,
              ln2_g, ln2_b):
    bsz, L, _ = x.shape
    x = layer_norm(x, ln_in_g, ln_in_b)
    c_act = jax.nn.silu(c)
    lb_cum = jnp.cumsum(jax.nn.softmax(hg_lb_logits.astype(jnp.float32), axis=0), axis=0)
    for l in range(DEPTH):
        mod = c_act @ w_ada[l] + b_ada[l]
        sh1, sc1, g1, sh2, sc2, g2 = [m[:, None, :] for m in jnp.split(mod, 6, axis=-1)]
        h = x * (1.0 + sc1) + sh1
        z = h @ w_in[l]
        a_u, a_v, b_cq, b_ckv, b_kr, c_u, d_q, d_f, d_i, d_g = jnp.split(z, IN_SPLITS, axis=-1)
        y_a = spatial_gating(jax.nn.gelu(a_u), jax.nn.gelu(a_v), gm_ln_g[l], gm_ln_b[l],
                             gm_ws[l], gm_bs[l])
        y_b = mla(b_cq, b_ckv, b_kr, mla_q_norm[l], mla_kv_norm[l], mla_w_uq[l], mla_w_ukv[l])
        y_c = s5(c_u, s5_a_re[l], s5_a_im[l], s5_b_re[l], s5_b_im[l], s5_c_re[l], s5_c_im[l],
                 s5_d[l], s5_log_step[l], s5_w_glu[l], s5_b_glu[l])
        y_d = hgrn2(d_q, d_f, d_i, d_g, lb_cum[l] - lb_cum[0], hg_norm_g[l])
        ym = jnp.concatenate([y_a, y_b, y_c, y_d], axis=-1).reshape(bsz, L, N_MIXERS, GROUP_WIDTH)
        ym = rms_norm(ym, merge_g[l].reshape(N_MIXERS, GROUP_WIDTH)).reshape(bsz, L, MIX_WIDTH)
        x = layer_norm(DN_ALPHA * x + (1.0 + g1) * (ym @ w_out[l]), ln1_g[l], ln1_b[l])
        h = x * (1.0 + sc2) + sh2
        x = layer_norm(DN_ALPHA * x + (1.0 + g2) * conv_ffn(h, w_up[l], conv_w[l], conv_b[l], w_down[l]),
                       ln2_g[l], ln2_b[l])
    return x


_drawn_inputs = setup_inputs


def setup_inputs(seed=0):
    import zlib

    import numpy as np

    out = dict(_drawn_inputs(seed))
    spreads = {}
    factors = {'gm_ln_g': 8.0,
     'gm_ln_b': 8.0,
     'gm_bs': 8.0,
     'mla_q_norm': 8.0,
     'mla_kv_norm': 8.0,
     's5_a_re': 8.0,
     's5_a_im': 3.016,
     's5_b_re': 4.33,
     's5_b_im': 4.031,
     's5_c_re': 4.291,
     's5_c_im': 4.048,
     's5_log_step': 3.363,
     's5_b_glu': 8.0,
     'hg_norm_g': 8.0,
     'merge_g': 5.38,
     'conv_b': 6.224}
    for name, (base, spread) in spreads.items():
        noise = np.random.default_rng([zlib.crc32(name.encode()), seed]).standard_normal(out[name].shape)
        drawn = base * np.exp(spread * noise) if base else spread * noise
        out[name] = __import__('jax').numpy.asarray(drawn.astype(out[name].dtype))
    for name, factor in factors.items():
        out[name] = (out[name] * factor).astype(out[name].dtype)
    return out
```

```python
from contextlib import ExitStack

import concourse.bass as bass
from concourse import mybir

F32 = mybir.dt.float32
I32 = mybir.dt.int32
ALU = mybir.AluOpType
ACT = mybir.ActivationFunctionType
AX_X = mybir.AxisListType.X

P = 128
D = 1024
T = 512
L = 2
KD = D // P
NB = T // P
CHUNK = 64
NCH = T // CHUNK
GW = 256
CT = GW // P
QR = 192
QH = QR // 2
ROPE = 32
NOPE = 64
QK = NOPE + ROPE
HEADS = 4
HD = 64
ST = 8
DFF = 2816
KF = DFF // P
NP2 = KF // 2
DK = KF // 2
ALPHA = (2 * L) ** 0.25
SCALE = float(QK) ** -0.5
LEVELS = [32, 16, 8, 4, 2, 1]
NEG = -1.0e30
MAGIC = 12582912.0
TWO_PI = 6.283185

MOD_A, MOD_B, MOD_C = 16, 24, 8
(U0, U1, F0, F1, Q0, Q1, I0, I1, G0, G1, CKV, CQ0, CQ1, AV0, AV1, AU0, AU1) = range(17)
NPROJ = 17


def chunk_order():
    order = [("ada", j) for j in range(MOD_A)]
    b = MOD_A
    for j in range(NPROJ):
        order.append(("win", j))
        for _ in range(2 if j < MOD_B - NPROJ else 1):
            order.append(("ada", b))
            b += 1
    order += [("out", m) for m in range(KD)]
    order += [("ada", b + m) for m in range(MOD_C)]
    order += [("up", m) for m in range(2 * KF)]
    order += [("down", m) for m in range(2 * KD)]
    return order


ORDER = chunk_order()
POS = {c: n for n, c in enumerate(ORDER)}
RING = 4
NCHUNK = len(ORDER)
NVIRT = -(-NCHUNK // RING) * RING
SLOT_TOTAL = [len(range(s, NCHUNK, RING)) for s in range(RING)]
SCRATCH = 26000
SLOT = DK * P

PA = [("b_ada", 48), ("gm_g", GW), ("gm_b", GW), ("gm_ws", HEADS * P), ("gm_bs", CT * P),
      ("q_norm", 2), ("kv_norm", 1), ("w_uq", 2 * HEADS * QK), ("w_uqs", 2 * HEADS * ROPE), ("w_ukv", 2 * GW),
      ("s5_are", CT * 64), ("s5_aim", CT * 64), ("s5_ls", CT * 64), ("s5_bre", CT * 64), ("s5_bim", CT * 64),
      ("s5_cre", ST * 16), ("s5_cim", ST * 16), ("s5_sre", ST), ("s5_sim", ST), ("s5_sls", ST),
      ("s5_d", CT), ("w_glu", CT * GW), ("b_glu", CT), ("hg_lb", CT * L), ("hg_sel", CT * L), ("hg_g", CT),
      ("merge", KD), ("ln1_g", KD), ("ln1_b", KD)]
PB = [("conv_w", 3 * 2 * KF), ("conv_b", 2 * KF), ("ln2_g", KD), ("ln2_b", KD), ("ln2_a", 1)]
CF = [("rope_c", T), ("rope_s", T), ("iota", T), ("reset", T), ("ident", P), ("ones", P), ("head", 2), ("nhead", 2),
      ("pair", 2), ("half_pi", 1), ("mask_q", P), ("mask_k", P), ("levels", 7 * P), ("c", KD), ("lng", KD), ("lnb", KD)]


def offsets(pack):
    at, o = {}, 0
    for name, n in pack:
        at[name] = (o, n)
        o += n
    return at, o


PA_AT, PA_N = offsets(PA)
PB_AT, PB_N = offsets(PB)
CF_AT, CF_N = offsets(CF)


def trunk(nc, x, consts, par_a, par_b, w_ada, w_in, w_out, w_up, w_down, out):
    ctx = ExitStack()
    with ctx:
        def sb(name, shape, dt=F32):
            return ctx.enter_context(nc.sbuf_tensor(name, shape, dt))

        banks = [ctx.enter_context(nc.psum_tensor(f"bank{i}", [P, T], F32)) for i in range(8)]

        xa = sb("xa", [P, KD, T])
        hm = sb("hm", [P, KD, T])
        ym = sb("ym", [P, KD, T])
        ring = sb("ring", [P, RING, SLOT])
        pa = sb("pa", [P, PA_N])
        pb = sb("pb", [P, PB_N])
        cf = sb("cf", [P, CF_N])
        silu_c = sb("silu_c", [P, KD])
        mod = sb("mod", [P, 48])
        s1c = sb("s1c", [P, KD])
        s2c = sb("s2c", [P, KD])
        g1p = sb("g1p", [P, KD])
        g2p = sb("g2p", [P, KD])
        ga = sb("ga", [P, 2, KD])
        st = sb("st", [P, 64])
        small = sb("small", [P, 96])
        scr = sb("scr", [P, SCRATCH])

        idle = sb("idle", [P, 128])

        taken = [0]

        def carve(n, at=None):
            a = taken[0] if at is None else at
            if at is None:
                taken[0] += n
            assert a + n <= SCRATCH, a + n
            return scr[:, a:a + n]

        def tiles(ap, n, w=T):
            return ap.rearrange("p (n w) -> p n w", w=w)

        sg = tiles(carve(CT * T), CT)
        qt = tiles(carve(CT * T), CT)
        vtok = tiles(carve(NB * GW), NB, GW)
        ckv = tiles(carve(T), 1)
        cq = tiles(carve(2 * T), 2)
        kro = tiles(carve(2 * T), 2)
        avt = tiles(carve(NB * GW), NB, GW)
        tab0 = taken[0]
        cos_t = tiles(carve(ST * T), ST)
        sin_t = tiles(carve(ST * T), ST)
        tab1 = taken[0]
        att = tiles(carve(HEADS * T, tab0), HEADS)
        sbd = tiles(carve(CT * NCH * P, tab0 + HEADS * T), CT * NCH, P)
        ketok = tiles(carve(CT * T, tab0 + HEADS * T + CT * NCH * P), CT)
        ee = tiles(carve(2 * T, tab0 + HEADS * T + CT * NCH * P + CT * T), 2)
        qh = tiles(carve(HEADS * T, tab0), HEADS)
        kt = tiles(carve(HEADS * T, tab0 + HEADS * T), HEADS)
        vb = tiles(carve(NB * GW, tab0 + 2 * HEADS * T), NB, GW)
        ptt = tiles(carve(2 * T, tab0 + 2 * HEADS * T + NB * GW), 2)
        assert tab0 + HEADS * T + CT * NCH * P + CT * T + 2 * T <= tab1
        s50 = taken[0]
        pin = tiles(carve(4 * T), 4)
        bp = tiles(carve(2 * T), 2)
        gg = tiles(carve(2 * T), 2)
        pout = tiles(carve(4 * T), 4)
        hh = tiles(carve(2 * T), 2)
        kc = tiles(carve(CT * T, s50), CT)
        bc = tiles(carve(CT * T, s50 + CT * T), CT)
        ke = tiles(carve(CT * T, s50 + 2 * CT * T), CT)
        qe = tiles(carve(CT * T, s50 + 3 * CT * T), CT)
        pp = tiles(carve(2 * T, s50 + 8 * T), 2)
        qk2 = tiles(carve(2 * T, s50 + 12 * T), 2)
        bd = carve(2 * CT * P).rearrange("p (r c n) -> p r c n", r=2, n=P)
        cbd = carve(2 * ST * 32).rearrange("p (r s n) -> p r s n", r=2, n=32)
        sp_ = carve(12 * P)
        dg = tiles(carve(2 * T), 2)
        hf = tiles(carve(KF * T, 0), KF)
        cv = tiles(carve(6 * T, KF * T), 6)
        assert (KF + 6) * T <= taken[0] - 2 * T

        def sems(*names):
            return {n: ctx.enter_context(nc.semaphore(n)) for n in names}

        landed = [ctx.enter_context(nc.semaphore(f"landed{i}")) for i in range(RING)]
        S = {
            **sems("const_in", "para_in", "parb_in", "x_in", "chunk_used", "layer_done", "mixers_done", "out_done"),
            **sems("dve_chain", "act_chain", "pool_chain"),
            **sems("silu_ready", "mod_a", "mod_b", "mod_c", "mod_ready", "ln_par", "ln_sq", "ln_stat", "ln_var", "ln_sd",
                   "ln_diag", "ln_bcast", "ln_normed", "ln_x", "h_ready", "resid_mm", "resid"),
            **sems("proj_mm", "proj_out"),
            **sems("s5_ang", "s5_trig", "s5_par", "s5_turn", "s5_tab", "s5_b", "s5_pin", "s5_bp", "s5_pout", "s5_h", "s5_c",
                   "s5_y", "s5_gelu", "s5_glu", "s5_gate", "s5_done"),
            **sems("hg_f", "hg_lnf", "hg_b", "hg_arg", "hg_exp", "hg_ke", "hg_ktr", "hg_ktok", "hg_u", "hg_s", "hg_zero",
                   "hg_larg", "hg_lexp", "hg_lqk", "hg_lmm", "hg_lcp", "hg_omm", "hg_osq", "hg_done"),
            **sems("r_sq", "r_stat", "r_var", "r_sd", "r_diag", "r_bcast", "r_used"),
            **sems("q_mm", "q_out", "k_mm", "k_out", "v_mm", "v_out", "sc_mm", "sc_max", "sc_exp", "sc_norm", "pt_mm", "pt_out",
                   "pv_mm", "mla_done"),
            **sems("gm_var", "gm_sd", "gm_vn", "gm_mm", "gm_done"),
            **sems("up_mm", "up_tap", "up_mid", "up_conv", "up_silu", "up_h"),
        }

        def p_a(name, a=0, n=None):
            o, w = PA_AT[name]
            return pa[:, o + a:o + (w if n is None else a + n)]

        def p_b(name, a=0, n=None):
            o, w = PB_AT[name]
            return pb[:, o + a:o + (w if n is None else a + n)]

        def c_f(name, a=0, n=None):
            o, w = CF_AT[name]
            return cf[:, o + a:o + (w if n is None else a + n)]

        ident = c_f("ident")
        ones = c_f("ones")
        level_mask = c_f("levels").bitcast(I32).rearrange("p (v t) -> p v t", t=P)
        block = ctx.enter_context(nc.Block())

        carry = {}
        carried = [0]

        def idle_col():
            carried[0] += 1
            return idle[:, carried[0] - 1:carried[0]]

        def wait_apart(eng, s, value):
            eng.wait_ge(s, value)
            carry[eng]()

        class Chain:

            def __init__(self, eng, s, per_layer):
                self.eng, self.s, self.per, self.l, self.n, self.base = eng, s, per_layer, 0, 0, 0

            def post(self, ins):
                self.n += 1
                ins.then_inc(self.s, 1)
                return ins

            def settle(self):
                self.eng.wait_ge(self.s, self.l * self.per + (self.base + self.n))

            def settle_apart(self):
                wait_apart(self.eng, self.s, self.l * self.per + (self.base + self.n))

            def link(self, ins):
                self.post(ins)
                self.settle()

            def layer(self, l):
                self.base, self.n, self.l = self.base + self.n, 0, l

            def close(self, ins):
                assert self.per > self.n, self.n
                ins.then_inc(self.s, self.per - self.n)

        @block.sync
        def _(sp):
            sp.dma_start(cf[:, :], consts).then_inc(S["const_in"], 16)
            sp.dma_start(xa[:, :, :], x).then_inc(S["x_in"], 16)
            with sp.Fori(0, L) as l:
                sp.wait_ge(S["mixers_done"], l + 1)
                sp.dma_start(pa[:, :], par_a[l]).then_inc(S["para_in"], 16)

                def load(n):
                    kind, j = ORDER[n]
                    sp.wait_ge(S["chunk_used"], l * NVIRT + (n + 1))
                    src = {"ada": w_ada, "win": w_in, "out": w_out, "up": w_up, "down": w_down}[kind]
                    w = SLOT if kind == "down" else KD * P
                    sp.dma_start(ring[:, n % RING, 0:w], src[l, j]).then_inc(landed[n % RING], 16)

                first_up = POS[("up", 0)]
                for n in range(first_up):
                    load(n)
                    if n == MOD_A + 4:
                        sp.wait_ge(S["layer_done"], l + 1)
                        sp.dma_start(pb[:, :], par_b[l]).then_inc(S["parb_in"], 16)
                used0 = sp.snap(l * NVIRT + (first_up + 1))
                with sp.Fori(0, NP2) as i:
                    used = sp.snap(used0 + i * 4)
                    need = [used] + [sp.snap(used + r) for r in range(1, 4)]
                    for r in range(4):
                        n = first_up + r
                        sp.wait_ge(S["chunk_used"], need[r])
                        sp.dma_start(ring[:, n % RING, 0:KD * P], w_up[l, i * 4 + r]).then_inc(landed[n % RING], 16)
                for n in range(POS[("down", 0)], NCHUNK):
                    load(n)
            sp.wait_ge(S["ln_x"], (2 * L + 1) * KD)
            sp.dma_start(out, xa[:, :, :]).then_inc(S["out_done"], 16)
            sp.wait_ge(S["out_done"], 16)

        @block.tensor
        def _(pe):
            mm = nc.tensor.matmul
            carry[pe] = lambda: mm(banks[7][:, 63:64], ones, ones[:, 0:1], start=True, stop=True)

            def chunk(l, n):
                need = l * (16 * SLOT_TOTAL[n % RING]) + 16 * (n // RING + 1)
                pe.wait_ge(landed[n % RING], need)
                return ring[:, n % RING, 0:SLOT].rearrange("p (k m) -> p k m", m=P)

            def row_stats(src, nk, rows, col, rhs):
                w = rhs.shape[-1]
                for b in range(NB):
                    for k in range(nk):
                        last = mm(banks[7][:, col + w * b:col + w * (b + 1)], src[0:rows, k, b * P:(b + 1) * P],
                                  rhs, start=(k == 0), stop=(k == nk - 1))
                return last

            def norm(n):
                pe.wait_ge(S["ln_sq"], n * KD)
                row_stats(xa, KD, P, 64, ones[:, 0:1])
                row_stats(hm, KD, P, 68, ones[:, 0:1]).then_inc(S["ln_stat"], 1)
                pe.wait_ge(S["ln_diag"], n)
                for r in range(2):
                    last = mm(banks[r][:, :], ones, dg[:, r, :], start=True, stop=True)
                last.then_inc(S["ln_bcast"], 1)

            def mod_cols(l, j0, j1, bank=7):
                for j in range(j0, j1):
                    w = chunk(l, POS[("ada", j)])
                    for k in range(KD):
                        last = mm(banks[bank][:, j:j + 1], w[:, k, :], silu_c[:, k:k + 1],
                                  start=(k == 0), stop=(k == KD - 1))
                        if k == 0:
                            last.then_inc(S["chunk_used"], 1)
                return last

            pe.wait_ge(S["const_in"], 16)
            mm(banks[7][:, 63:64], ones, ones[:, 0:1], start=True, stop=True).then_inc(S["chunk_used"], RING - 1)
            norm(1)
            pe.wait_ge(S["silu_ready"], 1)
            with pe.Fori(0, L) as l:
                mod_cols(l, 0, MOD_A).then_inc(S["mod_a"], 1)

                for k in range(KD):
                    pe.wait_ge(S["h_ready"], (2 * l) * KD + (k + 1))
                b_next = MOD_A

                def s5_b(t):
                    if t == 0:
                        pe.wait_ge(S["s5_par"], 1 + l)
                        pe.wait_ge(S["proj_out"], l * NPROJ + U1 + 1)
                    else:
                        pe.wait_ge(S["s5_pin"], l * ST + t)
                    c, q = t // 4, t % 4
                    rows = slice(32 * q, 32 * q + 32)
                    for r in range(2):
                        last = mm(banks[2 + r][:, :], bd[rows, r, c, :], ym[rows, 4 + c, :], start=True, stop=True,
                                  tile_position=(32 * q, 0))
                    last.then_inc(S["s5_b"], 1)

                def s5_c(t):
                    pe.wait_ge(S["s5_h"], l * ST + (t + 1))
                    c, q = t // 4, t % 4
                    rows = slice(32 * q, 32 * q + 32)
                    for r in range(2):
                        last = mm(banks[4 + c][rows, :], cbd[:, r, t, :], hh[:, r, :], start=(r == 0), stop=(r == 1))
                    last.then_inc(S["s5_c"], 1)

                for j in range(NPROJ):
                    w = chunk(l, POS[("win", j)])
                    if j >= 2:
                        pe.wait_ge(S["proj_out"], l * NPROJ + j - 1)
                    bank = banks[j % 2]
                    if j in (I0, I1, AV0, AV1):
                        for b in range(NB):
                            for k in range(KD):
                                last = mm(bank[:, b * P:(b + 1) * P], hm[:, k, b * P:(b + 1) * P], w[:, k, :],
                                          start=(k == 0), stop=(k == KD - 1))
                                if b == 0 and k == 0:
                                    last.then_inc(S["chunk_used"], 1)
                    elif j in (CQ0, CQ1):
                        if j == CQ1:
                            pe.wait_ge(S["proj_out"], l * NPROJ + CQ0 + 1)
                        for k in range(KD):
                            last = mm(bank[0:QH, :], w[:, k, 0:QH], hm[:, k, :], start=(k == 0), stop=(k == KD - 1))
                            if k == 0:
                                last.then_inc(S["chunk_used"], 1)
                        for k in range(KD):
                            last = mm(banks[6][NOPE:QK, :], w[:, k, QH:P], hm[:, k, :], start=(k == 0),
                                      stop=(k == KD - 1))
                    else:
                        for k in range(KD):
                            last = mm(bank[:, :], w[:, k, :], hm[:, k, :], start=(k == 0), stop=(k == KD - 1))
                            if k == 0:
                                last.then_inc(S["chunk_used"], 1)
                    last.then_inc(S["proj_mm"], 1)
                    n_b = 2 if j < MOD_B - NPROJ else 1
                    last = mod_cols(l, b_next, b_next + n_b)
                    if j == NPROJ - 1:
                        last.then_inc(S["mod_b"], 1)
                    b_next += n_b
                    if 3 <= j < 3 + ST:
                        s5_b(j - 3)
                    if 6 <= j < 6 + ST:
                        s5_c(j - 6)

                pe.wait_ge(S["s5_gelu"], l * CT + CT)
                pe.wait_ge(S["proj_out"], l * NPROJ + NPROJ)
                wg = p_a("w_glu").rearrange("p (k n) -> p k n", n=GW)
                for m in range(CT):
                    for k in range(CT):
                        last = mm(banks[m][:, :], wg[:, k, m * P:(m + 1) * P], ym[:, 4 + k, :], start=(k == 0),
                                  stop=(k == CT - 1))
                last.then_inc(S["s5_glu"], 1)

                pe.wait_ge(S["hg_ke"], l + 1)
                for c in range(CT):
                    for b in range(NB):
                        last = nc.tensor.transpose(banks[2 + c][:, b * P:(b + 1) * P], ke[:, c, b * P:(b + 1) * P], ident)
                last.then_inc(S["hg_ktr"], 1)
                pe.wait_ge(S["hg_ktok"], l + 1)
                pe.wait_ge(S["s5_y"], l * CT + CT)
                for c in range(CT):
                    if c:
                        pe.wait_ge(S["hg_s"], l * CT + 1)
                    for par in range(2):
                        rows = slice(64 * par, 64 * par + 64)
                        for b in range(NB):
                            last = mm(banks[4 + par][:, b * P:(b + 1) * P], ketok[rows, c, b * P:(b + 1) * P],
                                      vtok[rows, b, c * P:(c + 1) * P], start=True, stop=True)
                    last.then_inc(S["hg_u"], 1)
                step = 0
                for lv in range(len(LEVELS) + 1):
                    for c in range(CT):
                        if lv < len(LEVELS):
                            pe.wait_ge(S["hg_lqk"], l * (2 * len(LEVELS)) + step + 1)
                        if step == 0:
                            pe.wait_ge(S["s5_gate"], l + 1)
                        if step >= 2:
                            pe.wait_ge(S["hg_lcp"], l * 14 + step - 1)
                        for hp in range(2):
                            rows = slice(64 * hp, 64 * hp + 64)
                            for b in range(NB):
                                cols = slice(b * P, (b + 1) * P)
                                left = qk2[rows, c, cols] if lv < len(LEVELS) else kc[rows, c, cols]
                                right = qk2[rows, c, cols] if lv < len(LEVELS) else qt[rows, c, cols]
                                last = mm(banks[2 * (step % 2) + hp][:, cols], left, right, start=True, stop=True)
                        last.then_inc(S["hg_lmm"], 1)
                        step += 1
                pe.wait_ge(S["hg_lcp"], l * 14 + 14)
                pe.wait_ge(S["hg_s"], l * CT + CT)
                for c in range(CT):
                    for n in range(1, NCH):
                        mm(banks[4 + c][:, n * 64:(n + 1) * 64], sbd[:, c * NCH + n, :], qe[:, c, n * 64:(n + 1) * 64],
                           start=(n == 1), stop=False, skip_group_check=True)
                    for hp in range(2):
                        for b in range(NB):
                            h = 2 * c + hp
                            last = mm(banks[4 + c][64 * hp:64 * hp + 64, b * P:(b + 1) * P],
                                      vtok[:, b, h * HD:(h + 1) * HD], att[:, h, b * P:(b + 1) * P],
                                      start=False, stop=True, skip_group_check=True)
                last.then_inc(S["hg_omm"], 1)
                pe.wait_ge(S["hg_osq"], l + 1)
                for c in range(CT):
                    last = row_stats(ke[:, c:c + 1, :], 1, P, 80 + 2 * NB * c, c_f("head"))
                last.then_inc(S["r_stat"], 1)
                pe.wait_ge(S["r_diag"], l * 7 + 1)
                for h in range(2):
                    mm(banks[h // 2][64 * (h % 2):64 * (h % 2) + 64, :], ones[:, 0:64], dg[:, h, :], start=True, stop=True)\
                        .then_inc(S["r_bcast"], 1)
                pe.wait_ge(S["r_diag"], l * 7 + 2)
                for h in range(2, 4):
                    mm(banks[h // 2][64 * (h % 2):64 * (h % 2) + 64, :], ones[:, 0:64], dg[:, h - 2, :], start=True,
                       stop=True).then_inc(S["r_bcast"], 1)

                pe.wait_ge(S["r_sq"], l * 2 + 1)
                row_stats(ke, 2, QH, 72, ones[0:QH, 0:1])
                row_stats(qe[:, 0:1, :], 1, P, 76, ones[:, 0:1]).then_inc(S["r_stat"], 1)
                pe.wait_ge(S["r_diag"], l * 7 + 3)
                for r in range(2):
                    last = mm(banks[2 + r][:, :], ones, dg[:, r, :], start=True, stop=True)
                last.then_inc(S["r_bcast"], 1)
                pe.wait_ge(S["r_used"], l * 2 + 1)
                wq = p_a("w_uq").rearrange("p (k h m) -> p k h m", k=2, m=QK)
                ws = p_a("w_uqs").rearrange("p (k h m) -> p k h m", k=2, m=ROPE)
                for h in range(HEADS):
                    if h == 0:
                        pe.wait_ge(S["hg_done"], l + 1)
                    if h >= 2:
                        pe.wait_ge(S["q_out"], l * HEADS + h - 1)
                    for k in range(2):
                        mm(banks[2 * (h % 2)][0:QK, :], wq[0:QH, k, h, :], cq[0:QH, k, :], start=(k == 0), stop=(k == 1))
                    for k in range(2):
                        last = mm(banks[2 * (h % 2) + 1][NOPE:QK, :], ws[0:QH, k, h, :], cq[0:QH, k, :],
                                  start=(k == 0), stop=(k == 1))
                    last.then_inc(S["q_mm"], 1)
                wkv = p_a("w_ukv")
                for h in range(HEADS):
                    if h >= 2:
                        pe.wait_ge(S["k_out"], l * HEADS + h - 1)
                    mm(banks[4 + h % 2][0:NOPE, :], wkv[:, h * NOPE:(h + 1) * NOPE], ckv[:, 0, :], start=True, stop=True)\
                        .then_inc(S["k_mm"], 1)
                for b in range(NB):
                    if b == 1:
                        pe.wait_ge(S["k_out"], l * HEADS + HEADS)
                    if b >= 2:
                        pe.wait_ge(S["v_out"], l * NB + b - 1)
                    bank = banks[6] if b % 2 == 0 else banks[4]
                    mm(bank[:, 0:GW], ckv[:, 0, b * P:(b + 1) * P], wkv[:, GW:2 * GW], start=True, stop=True)\
                        .then_inc(S["v_mm"], 1)

                def scores(i):
                    h, b = i // NB, i % NB
                    if i == 0:
                        pe.wait_ge(S["q_out"], l * HEADS + HEADS)
                        pe.wait_ge(S["v_out"], l * NB + NB)
                        pe.wait_ge(S["k_out"], l * HEADS + HEADS)
                    if i >= 2:
                        pe.wait_ge(S["sc_exp"], l * 16 + i - 1)
                    mm(banks[i % 2][:, 0:(b + 1) * P], qh[0:QK, h, b * P:(b + 1) * P], kt[0:QK, h, 0:(b + 1) * P],
                       start=True, stop=False, skip_group_check=True)
                    mm(banks[i % 2][:, b * P:(b + 1) * P], c_f("mask_q")[0:1, :], c_f("mask_k")[0:1, :], start=False,
                       stop=True, skip_group_check=True).then_inc(S["sc_mm"], 1)

                def turn(i):
                    b = i % NB
                    pe.wait_ge(S["sc_norm"], l * 16 + i + 1)
                    if i >= 2:
                        pe.wait_ge(S["pt_out"], l * 16 + i - 1)
                    for k in range(b + 1):
                        last = nc.tensor.transpose(banks[2 + i % 2][:, k * P:(k + 1) * P], pp[:, i % 2, k * P:(k + 1) * P],
                                                   ident)
                    last.then_inc(S["pt_mm"], 1)

                def values(i):
                    h, b = i // NB, i % NB
                    pe.wait_ge(S["pt_out"], l * 16 + i + 1)
                    for k in range(b + 1):
                        last = mm(banks[4 + h // 2][64 * (h % 2):64 * (h % 2) + 64, b * P:(b + 1) * P],
                                  vb[:, k, h * HD:(h + 1) * HD], ptt[:, i % 2, k * P:(k + 1) * P],
                                  start=(k == 0), stop=(k == b))
                    last.then_inc(S["pv_mm"], 1)

                for i in range(16 + 2):
                    if i < 16:
                        scores(i)
                    if 1 <= i < 17:
                        turn(i - 1)
                    if i >= 2:
                        values(i - 2)

                pe.wait_ge(S["gm_vn"], l + 1)
                wsT = p_a("gm_ws").rearrange("p (h i) -> p h i", i=P)
                for c in range(CT):
                    for hp in range(2):
                        for b in range(NB):
                            h = 2 * c + hp
                            last = mm(banks[2 + c][64 * hp:64 * hp + 64, b * P:(b + 1) * P],
                                      avt[:, b, h * HD:(h + 1) * HD], wsT[:, h, :], start=True, stop=True)
                last.then_inc(S["gm_mm"], 1)

                pe.wait_ge(S["r_sq"], l * 2 + 2)
                for g in range(4):
                    last = row_stats(hm[:, 2 * g:2 * g + 2, :], 2, P, 96 + NB * g, ones[:, 0:1])
                last.then_inc(S["r_stat"], 1)
                for g in range(4):
                    pe.wait_ge(S["r_diag"], l * 7 + 4 + g)
                    mm(banks[g][:, :], ones, dg[:, g % 2, :], start=True, stop=True).then_inc(S["r_bcast"], 1)
                pe.wait_ge(S["r_used"], l * 2 + 2)
                for m in range(KD):
                    w = chunk(l, POS[("out", m)])
                    if m >= 4:
                        pe.wait_ge(S["resid"], (2 * l) * KD + m - 3)
                    for k in range(KD):
                        last = mm(banks[m % 4][:, :], w[:, k, :], ym[:, k, :], start=(k == 0), stop=(k == KD - 1))
                        if k == 0:
                            last.then_inc(S["chunk_used"], 1)
                    last.then_inc(S["resid_mm"], 1)
                mod_cols(l, MOD_A + MOD_B, 48, bank=6).then_inc(S["mod_c"], 1)
                norm(2 * l + 2)

                wait_apart(pe, S["h_ready"], (2 * l + 1) * KD + KD)
                first_up = POS[("up", 0)]
                with pe.Fori(0, NP2) as i:
                    for r in range(4):
                        n = first_up + r
                        pe.wait_ge(landed[n % RING],
                                   l * (16 * SLOT_TOTAL[n % RING]) + i * 16 + 16 * (n // RING + 1))
                        w = ring[:, n % RING, 0:KD * P].rearrange("p (k m) -> p k m", m=P)
                        pe.wait_ge(S["up_conv"], l * (2 * KF) + i * 4 + r + 1)
                        for k in range(KD):
                            last = mm(banks[2 + r][:, :], w[:, k, :], hm[:, k, :], start=(k == 0), stop=(k == KD - 1))
                            if k == 0:
                                last.then_inc(S["chunk_used"], 1)
                        last.then_inc(S["up_mm"], 1)

                pe.wait_ge(S["up_h"], l * KF + KF + 2)
                for m in range(KD):
                    for half in range(2):
                        w = chunk(l, POS[("down", 2 * m + half)])
                        if half == 0 and m >= 2:
                            pe.wait_ge(S["resid"], (2 * l + 1) * KD + m - 1)
                        for k in range(DK):
                            last = mm(banks[m % 2][:, :], w[:, k, :], hf[:, half * DK + k, :],
                                      start=(half == 0 and k == 0), stop=(half == 1 and k == DK - 1))
                            if k == 0:
                                last.then_inc(S["chunk_used"], 1)
                    last.then_inc(S["resid_mm"], 1)
                mm(banks[7][:, 63:64], ones, ones[:, 0:1], start=True, stop=True).then_inc(S["chunk_used"], NVIRT - NCHUNK)
                norm(2 * l + 3)

        @block.vector
        def _(v):
            V = nc.vector
            carry[v] = lambda: V.memset(idle_col(), 0.0)
            ch = Chain(v, S["dve_chain"], 1024)

            def norm(n):
                v.wait_ge(S["ln_stat"], n)
                mean, sq, var, rstd, mr = (st[:, 4 * i:4 * i + 4] for i in range(5))
                ch.post(V.tensor_scalar(mean, banks[7][:, 64:68], 1.0 / D, None, ALU.mult))
                ch.link(V.tensor_scalar(sq, banks[7][:, 68:72], 1.0 / D, 1e-5, ALU.mult, ALU.add))
                ch.link(V.tensor_tensor(var, mean, mean, ALU.mult))
                ch.link(V.tensor_tensor(var, sq, var, ALU.subtract))
                V.tensor_scalar(var, var, 1e-5, None, ALU.max).then_inc(S["ln_var"], 1)
                v.wait_ge(S["ln_sd"], n)
                ch.link(V.reciprocal(rstd, var))
                ch.link(V.tensor_tensor(mr, mean, rstd, ALU.mult))
                for b in range(NB):
                    ch.post(V.tensor_scalar(dg[:, 0, b * P:(b + 1) * P], ident, rstd[:, b:b + 1], None, ALU.mult))
                for b in range(NB):
                    ins = V.tensor_scalar(dg[:, 1, b * P:(b + 1) * P], ident, mr[:, b:b + 1], None, ALU.mult)
                ins.then_inc(S["ln_diag"], 1)
                v.wait_ge(S["ln_bcast"], n)
                for k in range(KD):
                    ch.post(V.tensor_tensor(xa[:, k, :], xa[:, k, :], banks[0][:, :], ALU.mult))
                ch.settle()
                for k in range(KD):
                    V.tensor_tensor(xa[:, k, :], xa[:, k, :], banks[1][:, :], ALU.subtract).then_inc(S["ln_normed"], 1)

            def rows_rstd(n_stat, n_sd, cols, width, inv_n, eps, dst):
                v.wait_ge(S["r_stat"], n_stat)
                V.tensor_scalar(st[:, dst:dst + width], banks[7][:, cols:cols + width], inv_n, eps, ALU.mult, ALU.add)\
                    .then_inc(S["r_var"], 1)
                v.wait_ge(S["r_sd"], n_sd)
                ch.link(V.reciprocal(st[:, dst:dst + width], st[:, dst:dst + width]))

            def diagonals(r, cols, last_inc):
                for b in range(NB):
                    ins = V.tensor_scalar(dg[:, r, b * P:(b + 1) * P], ident, st[:, cols[b]:cols[b] + 1], None, ALU.mult)
                if last_inc:
                    ins.then_inc(S["r_diag"], 1)

            v.wait_ge(S["const_in"], 16)
            V.tensor_scalar(ga[:, :, :], c_f("lng", 0, 2 * KD).rearrange("p (a b) -> p a b", a=2), ALPHA, None, ALU.mult)\
                .then_inc(S["ln_par"], 1)
            norm(1)
            V.memset(small[:, 88:89], 0.0).then_inc(S["up_conv"], 4)
            V.memset(small[:, 89:90], 0.0).then_inc(S["up_h"], 2)
            V.memset(small[:, 90:91], 0.0).then_inc(S["mixers_done"], 1)
            V.memset(small[:, 91:92], 0.0).then_inc(S["layer_done"], 1)
            with v.Fori(0, L) as l:
                ch.layer(l)
                v.wait_ge(S["ln_x"], (2 * l + 1) * KD)
                v.wait_ge(S["para_in"], 16 * l + 16)
                W = lambda i: sp_[:, i * P:(i + 1) * P]
                are, aim = p_a("s5_are"), p_a("s5_aim")
                v.wait_ge(S["s5_ang"], 3 * l + 1)
                ch.post(V.tensor_tensor(W(1), W(0), are, ALU.mult))
                ch.post(V.tensor_tensor(W(2), W(0), aim, ALU.mult))
                ch.post(V.tensor_tensor(small[:, 0:8], small[:, 24:32], p_a("s5_sre"), ALU.mult))
                ch.post(V.tensor_tensor(small[:, 8:16], small[:, 24:32], p_a("s5_sim"), ALU.mult))
                ch.settle()
                ch.post(V.tensor_scalar(W(2), W(2), 1.0 / 6.283185307179586, None, ALU.mult))
                ch.post(V.tensor_scalar(small[:, 8:16], small[:, 8:16], 1.0 / 6.283185307179586, None, ALU.mult))
                ch.settle()
                ch.link(V.tensor_scalar(W(3), W(2), MAGIC, None, ALU.add))
                ch.link(V.scalar_tensor_tensor(W(3), W(3), MAGIC, W(2), ALU.subtract, ALU.subtract))
                V.scalar_tensor_tensor(W(4), W(3), -1.0, W(3), ALU.mult, ALU.max).then_inc(S["s5_ang"], 1)
                v.wait_ge(S["s5_trig"], l + 1)
                ch.post(V.tensor_tensor(W(6), W(5), W(6), ALU.mult))
                ch.post(V.tensor_tensor(W(7), W(5), W(7), ALU.mult))
                ch.post(V.tensor_tensor(W(8), are, are, ALU.mult))
                ch.post(V.tensor_tensor(W(9), aim, aim, ALU.mult))
                ch.settle()
                ch.post(V.tensor_scalar(W(6), W(6), -1.0, None, ALU.add))
                ch.post(V.tensor_tensor(W(8), W(8), W(9), ALU.add))
                ch.settle()
                ch.post(V.reciprocal(W(8), W(8)))
                ch.post(V.tensor_tensor(W(9), W(6), are, ALU.mult))
                ch.post(V.tensor_tensor(W(10), W(7), aim, ALU.mult))
                ch.post(V.tensor_tensor(W(11), W(7), are, ALU.mult))
                ch.post(V.tensor_tensor(W(0), W(6), aim, ALU.mult))
                ch.settle()
                ch.post(V.tensor_tensor(W(9), W(9), W(10), ALU.add))
                ch.post(V.tensor_tensor(W(11), W(11), W(0), ALU.subtract))
                ch.settle()
                ch.post(V.tensor_tensor(W(9), W(9), W(8), ALU.mult))
                ch.post(V.tensor_tensor(W(11), W(11), W(8), ALU.mult))
                ch.settle()
                ch.post(V.tensor_tensor(W(1), W(9), p_a("s5_bre"), ALU.mult))
                ch.post(V.tensor_tensor(W(2), W(11), p_a("s5_bim"), ALU.mult))
                ch.post(V.tensor_tensor(W(3), W(9), p_a("s5_bim"), ALU.mult))
                ch.post(V.tensor_tensor(W(4), W(11), p_a("s5_bre"), ALU.mult))
                ch.settle()
                ch.post(V.tensor_tensor(W(1), W(1), W(2), ALU.subtract))
                ch.post(V.tensor_tensor(W(3), W(3), W(4), ALU.add))
                ch.settle()
                for r in range(2):
                    src = W(1 + 2 * r).rearrange("p (c n) -> p c n", c=CT)
                    for g in range(2):
                        ch.post(V.tensor_scalar(bd[:, r, :, 64 * g:64 * g + 64], src, c_f("pair", g, 1), None, ALU.mult))
                for r, nm in ((0, "s5_cre"), (1, "s5_cim")):
                    src = p_a(nm).rearrange("p (s n) -> p s n", n=16)
                    hd = "nhead" if r else "head"
                    for g in range(2):
                        ch.post(V.tensor_scalar(cbd[:, r, :, 16 * g:16 * g + 16], src, c_f(hd, g, 1), None, ALU.mult))
                wsT = p_a("gm_ws").rearrange("p (h i) -> p h i", i=P)
                ch.post(V.memset(wsT[64:128, :, 0:64], 0.0))
                lg = p_a("hg_lb").rearrange("p (c j) -> p c j", j=L)
                lb, omlb = small[:, 40:42], small[:, 42:44]
                ch.post(V.tensor_tensor(small[:, 44:46], lg[:, :, 0], lg[:, :, 1], ALU.max))
                ch.settle()
                for j in range(L):
                    ins = V.tensor_tensor(small[:, 46 + 2 * j:48 + 2 * j], lg[:, :, j], small[:, 44:46], ALU.subtract)
                ins.then_inc(S["s5_par"], 1)
                v.wait_ge(S["s5_ang"], 3 * l + 3)
                ch.link(V.tensor_tensor(small[:, 50:52], small[:, 46:48], small[:, 48:50], ALU.add))
                ch.link(V.reciprocal(small[:, 50:52], small[:, 50:52]))
                ch.link(V.tensor_tensor(small[:, 52:54], small[:, 48:50], small[:, 50:52], ALU.mult))
                sel = p_a("hg_sel").rearrange("p (c j) -> p c j", j=L)
                ch.link(V.tensor_tensor(lb, small[:, 52:54], sel[:, :, 1], ALU.mult))
                ch.link(V.tensor_scalar(omlb, lb, -1.0, 1.0, ALU.mult, ALU.add))

                v.wait_ge(S["mod_a"], l + 1)
                ch.post(V.tensor_tensor(mod[:, 0:16], banks[7][:, 0:16], p_a("b_ada", 0, 16), ALU.add))
                ch.settle()
                V.tensor_scalar(s1c[:, :], mod[:, 8:16], 1.0, 1.0 / ALPHA, ALU.add, ALU.mult).then_inc(S["mod_ready"], 1)

                def s5_in(t):
                    v.wait_ge(S["s5_b"], l * ST + t + 1)
                    v.wait_ge(S["s5_tab"], l * ST + t + 1)
                    if t:
                        v.wait_ge(S["s5_bp"], l * ST + t)
                    ch.post(V.tensor_tensor(pin[:, 0, :], banks[2][:, :], cos_t[:, t, :], ALU.mult))
                    ch.post(V.tensor_tensor(pin[:, 1, :], banks[3][:, :], sin_t[:, t, :], ALU.mult))
                    ch.post(V.tensor_tensor(pin[:, 2, :], banks[3][:, :], cos_t[:, t, :], ALU.mult))
                    ch.settle()
                    V.tensor_tensor(pin[:, 3, :], banks[2][:, :], sin_t[:, t, :], ALU.mult).then_inc(S["s5_pin"], 1)

                def s5_out(t):
                    v.wait_ge(S["s5_bp"], l * ST + t + 1)
                    if t:
                        v.wait_ge(S["s5_h"], l * ST + t)
                    mag = small[:, 32 + t:33 + t].to_broadcast([P, T])
                    for r in range(2):
                        ch.post(V.tensor_tensor_scan(gg[:, r, :], mag, bp[:, r, :], 0.0, ALU.mult, ALU.add))
                    ch.settle()
                    ch.post(V.tensor_tensor(pout[:, 0, :], gg[:, 0, :], cos_t[:, t, :], ALU.mult))
                    ch.post(V.tensor_tensor(pout[:, 1, :], gg[:, 1, :], sin_t[:, t, :], ALU.mult))
                    ch.post(V.tensor_tensor(pout[:, 2, :], gg[:, 1, :], cos_t[:, t, :], ALU.mult))
                    ch.settle()
                    V.tensor_tensor(pout[:, 3, :], gg[:, 0, :], sin_t[:, t, :], ALU.mult).then_inc(S["s5_pout"], 1)

                def s5_skip(c):
                    v.wait_ge(S["s5_c"], l * ST + 4 * c + 4)
                    V.scalar_tensor_tensor(ym[:, 4 + c, :], ym[:, 4 + c, :], p_a("s5_d", c, 1), banks[4 + c][:, :],
                                           ALU.mult, ALU.add).then_inc(S["s5_y"], 1)

                for t in range(ST + 1):
                    if t < ST:
                        s5_in(t)
                    if t:
                        s5_out(t - 1)
                s5_skip(0)
                s5_skip(1)
                v.wait_ge(S["mod_b"], l + 1)
                ch.post(V.tensor_tensor(mod[:, 16:40], banks[7][:, 16:40], p_a("b_ada", 16, 24), ALU.add))
                ch.settle()
                ch.post(V.tensor_scalar(g1p[:, :], mod[:, 16:24], 1.0, None, ALU.add))
                V.tensor_scalar(s2c[:, :], mod[:, 32:40], 1.0, 1.0 / ALPHA, ALU.add, ALU.mult).then_inc(S["mod_ready"], 1)
                V.tensor_scalar(ga[:, :, :], p_a("ln1_g", 0, 2 * KD).rearrange("p (a b) -> p a b", a=2), ALPHA, None,
                                ALU.mult).then_inc(S["ln_par"], 1)

                v.wait_ge(S["proj_out"], l * NPROJ + F1 + 1)
                for c in range(CT):
                    ch.post(V.tensor_scalar(bc[:, c, :], sg[:, c, :], omlb[:, c:c + 1], lb[:, c:c + 1], ALU.mult, ALU.add))
                ch.settle()
                for c in range(CT):
                    ch.post(V.tensor_scalar(kc[:, c, :], bc[:, c, :], -1.0, 1.0, ALU.mult, ALU.add))
                ch.settle()
                for c in range(CT):
                    ins = V.tensor_scalar(bc[:, c, :], bc[:, c, :], 2.0 ** -63, None, ALU.max)
                    ins.then_inc(S["hg_f"], 1)
                v.wait_ge(S["hg_lnf"], l + 1)
                for c in range(CT):
                    ch.post(V.tensor_tensor_scan(bc[:, c, :], c_f("reset"), sg[:, c, :], 0.0, ALU.mult, ALU.add))
                ch.settle()
                for c in range(CT):
                    b3 = bc[:, c, :].rearrange("p (n t) -> p n t", t=CHUNK)
                    ins = V.tensor_tensor(sg[:, c, :].rearrange("p (n t) -> p n t", t=CHUNK),
                                          b3[:, :, CHUNK - 1:CHUNK].to_broadcast([P, NCH, CHUNK]), b3, ALU.subtract)
                    ins.then_inc(S["hg_arg"], 1)
                v.wait_ge(S["hg_exp"], l + 1)
                dec = small[:, 56:72].rearrange("p (c n) -> p c n", c=CT)
                for c in range(CT):
                    ch.post(V.tensor_copy(dec[:, c, :], qe[:, c, :].rearrange("p (n t) -> p n t", t=CHUNK)[:, :, CHUNK - 1]))
                ch.post(V.tensor_tensor(ke[:, 0, :], ke[:, 0, :], kc[:, 0, :], ALU.mult))
                ch.settle()
                V.tensor_tensor(ke[:, 1, :], ke[:, 1, :], kc[:, 1, :], ALU.mult).then_inc(S["hg_ke"], 1)
                v.wait_ge(S["proj_out"], l * NPROJ + Q1 + 1)
                for c in range(CT):
                    ch.post(V.tensor_tensor(qe[:, c, :], qe[:, c, :], qt[:, c, :], ALU.mult))
                v.wait_ge(S["s5_gate"], l + 1)
                for c in range(CT):
                    ins = V.tensor_tensor(ym[:, 4 + c, :], ym[:, 4 + c, :], pout[:, c, :], ALU.mult)
                    ins.then_inc(S["s5_done"], 1)
                v.wait_ge(S["hg_zero"], l + 1)

                for c in range(CT):
                    v.wait_ge(S["hg_u"], l * CT + c + 1)
                    for n in range(1, NCH):
                        src_bank = banks[4 + (n - 1) % 2]
                        b = (n - 1) // 2
                        for hp in range(2):
                            r = slice(64 * hp, 64 * hp + 64)
                            new = sbd[r, c * NCH + n, 64 * hp:64 * hp + 64]
                            add = src_bank[r, b * P + 64 * hp:b * P + 64 * hp + 64]
                            if n == 1:
                                ins = V.tensor_copy(new, add)
                            else:
                                ins = V.scalar_tensor_tensor(new, sbd[r, c * NCH + n - 1, 64 * hp:64 * hp + 64],
                                                             dec[r, c, n - 1:n], add, ALU.mult, ALU.add)
                        if n < NCH - 1:
                            ch.link(ins)
                    ins.then_inc(S["hg_s"], 1)

                step = 0
                for lv in range(len(LEVELS) + 1):
                    for c in range(CT):
                        if lv < len(LEVELS):
                            w = LEVELS[lv]
                            idx = l * 12 + 2 * lv + c
                            b4 = bc[:, c, :].rearrange("p (n t) -> p n t", t=2 * w)
                            e4 = ee[:, c, :].rearrange("p (n t) -> p n t", t=2 * w)
                            ref = b4[:, :, w - 1:w].to_broadcast([P, T // (2 * w), w])
                            ch.post(V.tensor_tensor(e4[:, :, 0:w], ref, b4[:, :, 0:w], ALU.subtract))
                            ch.settle()
                            V.tensor_tensor(e4[:, :, w:2 * w], b4[:, :, w:2 * w], ref, ALU.subtract).then_inc(S["hg_larg"], 1)
                    for c in range(CT):
                        if lv < len(LEVELS):
                            w = LEVELS[lv]
                            e4 = ee[:, c, :].rearrange("p (n t) -> p n t", t=2 * w)
                            q4 = qk2[:, c, :].rearrange("p (n t) -> p n t", t=2 * w)
                            v.wait_ge(S["hg_lexp"], l * 12 + 2 * lv + c + 1)
                            if lv:
                                v.wait_ge(S["hg_lmm"], l * 14 + 2 * (lv - 1) + c + 1)
                            ch.post(V.tensor_tensor(q4[:, :, 0:w], e4[:, :, 0:w],
                                                    kc[:, c, :].rearrange("p (n t) -> p n t", t=2 * w)[:, :, 0:w], ALU.mult))
                            ch.settle()
                            V.tensor_tensor(q4[:, :, w:2 * w], e4[:, :, w:2 * w],
                                            qt[:, c, :].rearrange("p (n t) -> p n t", t=2 * w)[:, :, w:2 * w],
                                            ALU.mult).then_inc(S["hg_lqk"], 1)
                    for c in range(CT):
                        wait_apart(v, S["hg_lmm"], l * 14 + step + 1)
                        for hp in range(2):
                            a3 = att[:, 2 * c + hp, :].rearrange("p (b t) -> p b t", t=P)
                            ins = V.copy_predicated(a3, level_mask[:, lv:lv + 1, :].to_broadcast([P, NB, P]),
                                                    banks[2 * (step % 2) + hp][:, :].rearrange("p (b t) -> p b t", t=P))
                        ins.then_inc(S["hg_lcp"], 1)
                        step += 1
                rows_rstd(l * 3 + 1, l * 3 + 1, 80, 16, 1.0 / HD, 1e-6, 24)
                for c in range(CT):
                    for hp in range(2):
                        diagonals(hp, [24 + 8 * c + 2 * b + hp for b in range(NB)], hp == 1)
                    v.wait_ge(S["r_bcast"], l * 9 + 2 * c + 2)
                for c in range(CT):
                    ch.post(V.scalar_tensor_tensor(ym[:, 6 + c, :], ym[:, 6 + c, :], p_a("hg_g", c, 1), banks[c][:, :],
                                                   ALU.mult, ALU.mult))
                ch.settle()
                ch.post(V.tensor_tensor(ym[:, 6, :], ym[:, 6, :], banks[4][:, :], ALU.mult))
                ch.settle()
                V.tensor_tensor(ym[:, 7, :], ym[:, 7, :], banks[5][:, :], ALU.mult).then_inc(S["hg_done"], 1)

                v.wait_ge(S["r_stat"], l * 3 + 2)
                ch.post(V.tensor_scalar(st[:, 40:44], banks[7][:, 72:76], 1.0 / QR, 1e-6, ALU.mult, ALU.add))
                ch.settle()
                V.tensor_scalar(st[:, 44:48], banks[7][:, 76:80], 1.0 / P, 1e-6, ALU.mult, ALU.add).then_inc(S["r_var"], 1)
                v.wait_ge(S["r_sd"], l * 3 + 2)
                ch.link(V.reciprocal(st[:, 40:48], st[:, 40:48]))
                diagonals(0, [40, 41, 42, 43], False)
                diagonals(1, [44, 45, 46, 47], True)
                v.wait_ge(S["r_bcast"], l * 9 + 5)
                for k in range(2):
                    ch.post(V.scalar_tensor_tensor(cq[0:QH, k, :], cq[0:QH, k, :], p_a("q_norm", k, 1)[0:QH, :],
                                                   banks[2][0:QH, :], ALU.mult, ALU.mult))
                ch.settle()
                V.scalar_tensor_tensor(ckv[:, 0, :], ckv[:, 0, :], p_a("kv_norm"), banks[3][:, :], ALU.mult, ALU.mult)\
                    .then_inc(S["r_used"], 1)
                kk, ks = kro[NOPE:QK, 0, :], kro[NOPE:QK, 1, :]
                ch.post(V.tensor_tensor(kk, kk, c_f("rope_c")[NOPE:QK, :], ALU.mult))
                ch.post(V.tensor_tensor(ks, ks, c_f("rope_s")[NOPE:QK, :], ALU.mult))
                ch.settle()
                for h in range(HEADS):
                    ch.post(V.tensor_tensor(kt[NOPE:QK, h, :], kk, ks, ALU.add))
                for h in range(HEADS):
                    v.wait_ge(S["q_mm"], l * HEADS + h + 1)
                    ch.post(V.tensor_tensor(qh[0:QK, h, :], banks[2 * (h % 2)][0:QK, :], c_f("rope_c")[0:QK, :], ALU.mult))
                    ch.post(V.tensor_tensor(ptt[NOPE:QK, h % 2, :], banks[2 * (h % 2) + 1][NOPE:QK, :],
                                            c_f("rope_s")[NOPE:QK, :], ALU.mult))
                    ch.settle()
                    V.tensor_tensor(qh[NOPE:QK, h, :], qh[NOPE:QK, h, :], ptt[NOPE:QK, h % 2, :], ALU.add)\
                        .then_inc(S["q_out"], 1)

                def softmax_max(i):
                    b = i % NB
                    v.wait_ge(S["sc_mm"], l * 16 + i + 1)
                    ch.link(V.tensor_reduce(st[:, 48 + i % 2:49 + i % 2], banks[i % 2][:, 0:(b + 1) * P], AX_X, ALU.max))
                    if i >= 2:
                        v.wait_ge(S["sc_exp"], l * 16 + i - 1)
                    V.tensor_scalar(st[:, 50 + i % 2:51 + i % 2], st[:, 48 + i % 2:49 + i % 2], -SCALE, None, ALU.mult).then_inc(S["sc_max"], 1)

                def softmax_norm(i):
                    b = i % NB
                    v.wait_ge(S["sc_exp"], l * 16 + i + 1)
                    ch.link(V.reciprocal(st[:, 54 + i % 2:55 + i % 2], st[:, 52 + i % 2:53 + i % 2]))
                    V.tensor_scalar(pp[:, i % 2, 0:(b + 1) * P], pp[:, i % 2, 0:(b + 1) * P], st[:, 54 + i % 2:55 + i % 2],
                                    None, ALU.mult).then_inc(S["sc_norm"], 1)

                for i in range(17):
                    if i < 16:
                        softmax_max(i)
                    if i:
                        softmax_norm(i - 1)

                v.wait_ge(S["proj_out"], l * NPROJ + AV1 + 1)
                bn = small[:, 0:24].rearrange("p (b s) -> p b s", b=NB)
                ag = small[:, 24:32].rearrange("p (b s) -> p b s", b=NB)
                v.wait_ge(S["s5_h"], l * ST + ST)
                for b in range(NB):
                    ch.post(V.bn_stats(bn[:, b, :], avt[:, b, :]))
                ch.settle_apart()
                for b in range(NB):
                    ch.post(V.bn_aggr(ag[:, b, :], bn[:, b, :]))
                ch.settle()
                V.tensor_scalar(st[:, 56:60], ag[:, :, 1], 1e-5, None, ALU.add).then_inc(S["gm_var"], 1)
                v.wait_ge(S["gm_sd"], l + 1)
                ch.link(V.reciprocal(st[:, 56:60], st[:, 56:60]))
                for b in range(NB):
                    ch.post(V.tensor_scalar(avt[:, b, :], avt[:, b, :], ag[:, b, 0:1], st[:, 56 + b:57 + b], ALU.subtract,
                                            ALU.mult))
                ch.settle()
                for b in range(NB):
                    ch.post(V.tensor_tensor(avt[:, b, :], avt[:, b, :], p_a("gm_g"), ALU.mult))
                ch.settle()
                for b in range(NB):
                    ins = V.tensor_tensor(avt[:, b, :], avt[:, b, :], p_a("gm_b"), ALU.add)
                ins.then_inc(S["gm_vn"], 1)
                v.wait_ge(S["gm_mm"], l + 1)
                for c in range(CT):
                    for b in range(NB):
                        cols = slice(b * P, (b + 1) * P)
                        ch.post(V.tensor_tensor(kc[:, c, cols], banks[2 + c][:, cols], p_a("gm_bs", c * P, P), ALU.add))
                ch.settle()
                v.wait_ge(S["proj_out"], l * NPROJ + NPROJ)
                for c in range(CT):
                    ins = V.tensor_tensor(ym[:, c, :], ym[:, c, :], kc[:, c, :], ALU.mult)
                    ins.then_inc(S["gm_done"], 1)

                rows_rstd(l * 3 + 3, l * 3 + 3, 96, 16, 1.0 / GW, 1e-6, 24)
                for g in range(4):
                    if g >= 2:
                        v.wait_ge(S["r_bcast"], l * 9 + 5 + g - 1)
                    diagonals(g % 2, [24 + 4 * g + b for b in range(NB)], True)
                for g in range(4):
                    v.wait_ge(S["r_bcast"], l * 9 + 5 + g + 1)
                    for c in range(2):
                        ins = V.scalar_tensor_tensor(ym[:, 2 * g + c, :], ym[:, 2 * g + c, :], p_a("merge", 2 * g + c, 1),
                                                     banks[g][:, :], ALU.mult, ALU.mult)
                ins.then_inc(S["r_used"], 1)
                for m in range(KD):
                    v.wait_ge(S["resid_mm"], (2 * l) * KD + m + 1)
                    V.scalar_tensor_tensor(xa[:, m, :], banks[m % 4][:, :], g1p[:, m:m + 1], xa[:, m, :], ALU.mult, ALU.add)\
                        .then_inc(S["resid"], 1)
                v.wait_ge(S["mod_c"], l + 1)
                ch.post(V.tensor_tensor(mod[:, 40:48], banks[6][:, 40:48], p_a("b_ada", 40, 8), ALU.add))
                ch.settle()
                V.tensor_scalar(g2p[:, :], mod[:, 40:48], 1.0, None, ALU.add).then_inc(S["mixers_done"], 1)
                norm(2 * l + 2)
                v.wait_ge(S["parb_in"], 16 * l + 16)
                v.wait_ge(S["ln_x"], (2 * l + 2) * KD)
                V.tensor_scalar(ga[:, :, :], p_b("ln2_g", 0, 2 * KD).rearrange("p (a b) -> p a b", a=2), p_b("ln2_a"),
                                None, ALU.mult).then_inc(S["ln_par"], 1)

                with v.Fori(0, NP2) as i:
                    o = PB_AT["conv_w"][0]
                    for r in range(4):
                        m = i * 4 + r
                        v.wait_ge(S["up_tap"], l * (2 * KF) + i * 4 + r + 1)
                        dst, bank = cv[:, r, :], banks[2 + r]
                        V.scalar_tensor_tensor(dst[:, 1:T], bank[:, 0:T - 1], pb[:, bass.ds(m * 3 + (o + 1), 1)],
                                               dst[:, 1:T], ALU.mult, ALU.add).then_inc(S["up_mid"], 1)
                        v.wait_ge(S["up_mid"], l * (2 * KF) + i * 4 + (r + 1))
                        V.scalar_tensor_tensor(dst[:, 2:T], bank[:, 0:T - 2], pb[:, bass.ds(m * 3 + o, 1)],
                                               dst[:, 2:T], ALU.mult, ALU.add).then_inc(S["up_conv"], 1)
                        if r % 2:
                            v.wait_ge(S["up_silu"], l * KF + i * 2 + (r // 2 + 1))
                            V.tensor_tensor(hf[:, bass.ds(i * 2 + r // 2, 1), :].rearrange("p a t -> p (a t)"),
                                            cv[:, r - 1, :], cv[:, 4 + r // 2, :], ALU.mult).then_inc(S["up_h"], 1)
                for m in range(KD):
                    v.wait_ge(S["resid_mm"], (2 * l + 1) * KD + m + 1)
                    V.scalar_tensor_tensor(xa[:, m, :], banks[m % 2][:, :], g2p[:, m:m + 1], xa[:, m, :], ALU.mult, ALU.add)\
                        .then_inc(S["resid"], 1)
                norm(2 * l + 3)
                V.memset(small[:, 94:95], 0.0).then_inc(S["layer_done"], 1)
                ch.close(V.memset(idle_col(), 0.0))

        @block.scalar
        def _(a):
            A = nc.scalar.activation
            carry[a] = lambda: A(idle_col(), c_f("half_pi"), ACT.Identity)
            ch = Chain(a, S["act_chain"], 256)

            def norm(n, sources):
                for k in range(KD):
                    if sources is not None:
                        a.wait_ge(S["resid"], sources + (k + 1))
                    A(hm[:, k, :], xa[:, k, :], ACT.Square).then_inc(S["ln_sq"], 1)
                a.wait_ge(S["ln_var"], n)
                A(st[:, 8:12], st[:, 8:12], ACT.Sqrt).then_inc(S["ln_sd"], 1)
                a.wait_ge(S["ln_par"], n)
                for k in range(KD):
                    a.wait_ge(S["ln_normed"], (n - 1) * KD + (k + 1))
                    A(xa[:, k, :], xa[:, k, :], ACT.Identity, scale=ga[:, 0, k:k + 1], bias=ga[:, 1, k:k + 1])\
                        .then_inc(S["ln_x"], 1)

            a.wait_ge(S["const_in"], 16)
            A(silu_c[:, :], c_f("c"), ACT.Silu).then_inc(S["silu_ready"], 1)
            a.wait_ge(S["x_in"], 16)
            norm(1, None)
            with a.Fori(0, L) as l:
                ch.layer(l)
                W = lambda i: sp_[:, i * P:(i + 1) * P]
                a.wait_ge(S["para_in"], 16 * l + 16)
                A(W(0), p_a("s5_ls"), ACT.Exp)
                A(small[:, 24:32], p_a("s5_sls"), ACT.Exp).then_inc(S["s5_ang"], 1)
                a.wait_ge(S["s5_ang"], 3 * l + 2)
                A(W(5), W(1), ACT.Exp)
                A(small[:, 32:40], small[:, 0:8], ACT.Exp)
                A(W(6), W(4), ACT.Sin, scale=-TWO_PI, bias=c_f("half_pi"))
                A(W(7), W(3), ACT.Sin, scale=-TWO_PI).then_inc(S["s5_trig"], 1)
                for t in range(ST):
                    a.wait_ge(S["s5_turn"], l * ST + t + 1)
                    ch.link(A(cos_t[:, t, :], sin_t[:, t, :], ACT.Abs))
                    A(sin_t[:, t, :], sin_t[:, t, :], ACT.Sin, scale=-TWO_PI)
                    A(cos_t[:, t, :], cos_t[:, t, :], ACT.Sin, scale=-TWO_PI, bias=c_f("half_pi")).then_inc(S["s5_tab"], 1)
                a.wait_ge(S["s5_par"], l + 1)
                A(small[:, 46:50], small[:, 46:50], ACT.Exp).then_inc(S["s5_ang"], 1)

                for j in range(NPROJ):
                    a.wait_ge(S["proj_mm"], l * NPROJ + j + 1)
                    bank = banks[j % 2]
                    tok = bank[:, :].rearrange("p (b n) -> p b n", n=P)
                    if j in (U0, U1):
                        A(ym[:, 4 + j - U0, :], bank[:, :], ACT.Identity).then_inc(S["proj_out"], 1)
                    elif j in (F0, F1):
                        A(sg[:, j - F0, :], bank[:, :], ACT.Sigmoid).then_inc(S["proj_out"], 1)
                    elif j in (Q0, Q1):
                        A(qt[:, j - Q0, :], bank[:, :], ACT.Identity).then_inc(S["proj_out"], 1)
                    elif j in (I0, I1):
                        A(vtok[:, :, (j - I0) * P:(j - I0 + 1) * P], tok, ACT.Identity).then_inc(S["proj_out"], 1)
                    elif j in (G0, G1):
                        A(ym[:, 6 + j - G0, :], bank[:, :], ACT.Sigmoid).then_inc(S["proj_out"], 1)
                    elif j == CKV:
                        A(ckv[:, 0, :], bank[:, :], ACT.Identity).then_inc(S["proj_out"], 1)
                    elif j in (CQ0, CQ1):
                        A(cq[0:QH, j - CQ0, :], bank[0:QH, :], ACT.Identity)
                        A(kro[NOPE:QK, j - CQ0, :], banks[6][NOPE:QK, :], ACT.Identity).then_inc(S["proj_out"], 1)
                    elif j in (AV0, AV1):
                        A(avt[:, :, (j - AV0) * P:(j - AV0 + 1) * P], tok, ACT.Gelu_apprx_tanh).then_inc(S["proj_out"], 1)
                    else:
                        A(ym[:, j - AU0, :], bank[:, :], ACT.Gelu_apprx_tanh).then_inc(S["proj_out"], 1)
                for c in range(CT):
                    a.wait_ge(S["s5_y"], l * CT + c + 1)
                    A(ym[:, 4 + c, :], ym[:, 4 + c, :], ACT.Gelu_apprx_tanh).then_inc(S["s5_gelu"], 1)
                a.wait_ge(S["s5_glu"], l + 1)
                A(pout[:, 0, :], banks[0][:, :], ACT.Sigmoid, bias=p_a("b_glu", 0, 1))
                A(pout[:, 1, :], banks[1][:, :], ACT.Sigmoid, bias=p_a("b_glu", 1, 1)).then_inc(S["s5_gate"], 1)

                a.wait_ge(S["hg_f"], l * CT + CT)
                A(sg[:, 0, :], bc[:, 0, :], ACT.Ln)
                A(sg[:, 1, :], bc[:, 1, :], ACT.Ln).then_inc(S["hg_lnf"], 1)
                a.wait_ge(S["hg_arg"], l * CT + CT)
                for c in range(CT):
                    A(ke[:, c, :], sg[:, c, :], ACT.Exp)
                A(qe[:, 0, :], bc[:, 0, :], ACT.Exp)
                A(qe[:, 1, :], bc[:, 1, :], ACT.Exp).then_inc(S["hg_exp"], 1)
                a.wait_ge(S["hg_ktr"], l + 1)
                A(ketok[:, 0, :], banks[2][:, :], ACT.Identity)
                A(ketok[:, 1, :], banks[3][:, :], ACT.Identity).then_inc(S["hg_ktok"], 1)
                for s in range(2 * len(LEVELS)):
                    a.wait_ge(S["hg_larg"], l * 12 + s + 1)
                    A(ee[:, s % 2, :], ee[:, s % 2, :], ACT.Exp).then_inc(S["hg_lexp"], 1)
                a.wait_ge(S["hg_omm"], l + 1)
                A(ke[:, 0, :], banks[4][:, :], ACT.Square)
                A(ke[:, 1, :], banks[5][:, :], ACT.Square).then_inc(S["hg_osq"], 1)
                a.wait_ge(S["r_var"], l * 3 + 1)
                A(st[:, 24:40], st[:, 24:40], ACT.Sqrt).then_inc(S["r_sd"], 1)

                a.wait_ge(S["r_stat"], l * 3 + 1)
                A(ke[0:QH, 0, :], cq[0:QH, 0, :], ACT.Square)
                A(ke[0:QH, 1, :], cq[0:QH, 1, :], ACT.Square)
                A(qe[:, 0, :], ckv[:, 0, :], ACT.Square).then_inc(S["r_sq"], 1)
                a.wait_ge(S["r_var"], l * 3 + 2)
                A(st[:, 40:48], st[:, 40:48], ACT.Sqrt).then_inc(S["r_sd"], 1)
                for h in range(HEADS):
                    a.wait_ge(S["k_mm"], l * HEADS + h + 1)
                    A(kt[0:NOPE, h, :], banks[4 + h % 2][0:NOPE, :], ACT.Identity).then_inc(S["k_out"], 1)
                for b in range(NB):
                    a.wait_ge(S["v_mm"], l * NB + b + 1)
                    A(vb[:, b, :], (banks[6] if b % 2 == 0 else banks[4])[:, 0:GW], ACT.Identity).then_inc(S["v_out"], 1)

                def soft_exp(i):
                    b = i % NB
                    a.wait_ge(S["sc_max"], l * 16 + i + 1)
                    if i >= 2:
                        a.wait_ge(S["pt_mm"], l * 16 + i - 1)
                        a.wait_ge(S["sc_norm"], l * 16 + i - 1)
                    A(pp[:, i % 2, 0:(b + 1) * P], banks[i % 2][:, 0:(b + 1) * P], ACT.Exp, scale=SCALE,
                      bias=st[:, 50 + i % 2:51 + i % 2], accum_out=st[:, 52 + i % 2:53 + i % 2]).then_inc(S["sc_exp"], 1)

                def turned(i):
                    b = i % NB
                    a.wait_ge(S["pt_mm"], l * 16 + i + 1)
                    if i >= 2:
                        a.wait_ge(S["pv_mm"], l * 16 + i - 1)
                    A(ptt[:, i % 2, 0:(b + 1) * P], banks[2 + i % 2][:, 0:(b + 1) * P], ACT.Identity).then_inc(S["pt_out"], 1)

                for i in range(17):
                    if i < 16:
                        soft_exp(i)
                    if i:
                        turned(i - 1)
                a.wait_ge(S["pv_mm"], l * 16 + 16)
                for c in range(CT):
                    A(ym[:, 2 + c, :], banks[4 + c][:, :], ACT.Identity).then_inc(S["mla_done"], 1)

                a.wait_ge(S["gm_var"], l + 1)
                A(st[:, 56:60], st[:, 56:60], ACT.Sqrt).then_inc(S["gm_sd"], 1)
                a.wait_ge(S["mla_done"], l * CT + CT)
                a.wait_ge(S["s5_done"], l * CT + CT)
                a.wait_ge(S["hg_done"], l + 1)
                for k in (2, 3, 4, 5, 6, 7):
                    A(hm[:, k, :], ym[:, k, :], ACT.Square)
                a.wait_ge(S["gm_done"], l * CT + CT)
                A(hm[:, 0, :], ym[:, 0, :], ACT.Square)
                A(hm[:, 1, :], ym[:, 1, :], ACT.Square).then_inc(S["r_sq"], 1)
                a.wait_ge(S["r_var"], l * 3 + 3)
                A(st[:, 24:40], st[:, 24:40], ACT.Sqrt).then_inc(S["r_sd"], 1)
                a.wait_ge(S["r_used"], l * 2 + 2)
                norm(2 * l + 2, (2 * l) * KD)

                o, ob = PB_AT["conv_w"][0], PB_AT["conv_b"][0]
                with a.Fori(0, NP2) as i:
                    for r in range(4):
                        m = i * 4 + r
                        a.wait_ge(S["up_h"], l * KF + i * 2 + (r // 2 + 1))
                        wait_apart(a, S["up_mm"], l * (2 * KF) + i * 4 + r + 1)
                        A(cv[:, r, :], banks[2 + r][:, :], ACT.Identity, scale=pb[:, bass.ds(m * 3 + (o + 2), 1)],
                          bias=pb[:, bass.ds(m + ob, 1)]).then_inc(S["up_tap"], 1)
                        if r % 2:
                            a.wait_ge(S["up_conv"], l * (2 * KF) + i * 4 + r + 1 + 4)
                            A(cv[:, 4 + r // 2, :], cv[:, r, :], ACT.Silu).then_inc(S["up_silu"], 1)
                norm(2 * l + 3, (2 * l + 1) * KD)
                ch.close(A(idle_col(), c_f("half_pi"), ACT.Identity))

        @block.gpsimd
        def _(g):
            G = nc.gpsimd
            carry[g] = lambda: G.tensor_tensor(idle_col(), c_f("half_pi"), c_f("half_pi"), ALU.add)
            g.wait_ge(S["const_in"], 16)
            ch = Chain(g, S["pool_chain"], 64)

            def modulate(l, which, scale, shift):
                for k in range(KD):
                    if k == 0:
                        g.wait_ge(S["mod_ready"], 2 * l + (which + 1))
                    wait_apart(g, S["ln_x"], (2 * l + which) * KD + (k + 1))
                    G.tensor_scalar(hm[:, k, :], xa[:, k, :], scale[:, k:k + 1], shift[:, k:k + 1], ALU.mult, ALU.add)\
                        .then_inc(S["h_ready"], 1)

            with g.Fori(0, L) as l:
                ch.layer(l)
                wait_apart(g, S["s5_ang"], 3 * l + 2)
                for t in range(ST):
                    ch.post(G.tensor_scalar(cos_t[:, t, :], c_f("iota"), small[:, 8 + t:9 + t], 0.0, ALU.mult, ALU.add))
                    ch.settle_apart()
                    ch.post(G.tensor_scalar(sin_t[:, t, :], cos_t[:, t, :], 1.0, MAGIC, ALU.mult, ALU.add))
                    ch.settle_apart()
                    ch.link(G.tensor_scalar(sin_t[:, t, :], sin_t[:, t, :], 1.0, -MAGIC, ALU.mult, ALU.add))
                    G.tensor_tensor(sin_t[:, t, :], sin_t[:, t, :], cos_t[:, t, :], ALU.subtract).then_inc(S["s5_turn"], 1)
                modulate(l, 0, s1c, mod[:, 0:8])

                def add_in(t):
                    g.wait_ge(S["s5_pin"], l * ST + (t + 1))
                    if t:
                        g.wait_ge(S["s5_pout"], l * ST + t)
                    G.tensor_tensor(bp[:, 0, :], pin[:, 0, :], pin[:, 1, :], ALU.add)
                    G.tensor_tensor(bp[:, 1, :], pin[:, 2, :], pin[:, 3, :], ALU.subtract).then_inc(S["s5_bp"], 1)

                def add_out(t):
                    g.wait_ge(S["s5_pout"], l * ST + (t + 1))
                    if t:
                        g.wait_ge(S["s5_c"], l * ST + t)
                    G.tensor_tensor(hh[:, 0, :], pout[:, 0, :], pout[:, 1, :], ALU.subtract)
                    G.tensor_tensor(hh[:, 1, :], pout[:, 2, :], pout[:, 3, :], ALU.add).then_inc(S["s5_h"], 1)

                for t in range(ST + 1):
                    if t < ST:
                        add_in(t)
                    if t:
                        add_out(t - 1)
                G.memset(att[:, :, :], 0.0)
                G.memset(sbd[:, :, :], 0.0).then_inc(S["hg_zero"], 1)
                modulate(l, 1, s2c, mod[:, 24:32])
                ch.close(G.memset(idle_col(), 0.0))


def kernel(**inputs):
    import numpy as np
    import concourse.bacc as _bacc
    from concourse.bass_utils import run_bass_kernel_spmd as _run

    a = {k: np.asarray(v) for k, v in inputs.items()}

    def cols(v):
        return np.swapaxes(v.reshape(*v.shape[:-1], -1, P), -1, -2)

    def chunks(w, nk=KD):
        n = w.shape[2] // P
        return w.reshape(L, nk, P, n, P).transpose(0, 3, 2, 1, 4)

    wi = a["w_in"]
    sizes = (GW, GW, QR, P, ROPE, GW, GW, GW, GW, GW)
    at = np.cumsum((0,) + sizes)
    au, av, cq, ckv, kr, cu, dq, df, di, dg = (wi[:, :, at[i]:at[i + 1]] for i in range(10))
    krs = np.concatenate([kr[:, :, ROPE // 2:], kr[:, :, :ROPE // 2]], 2)
    win = np.concatenate([cu, df, dq, di, dg, ckv, cq[:, :, :QH], kr, cq[:, :, QH:], krs, av, au], 2)
    up = a["w_up"].reshape(L, D, 2, KF, P).transpose(0, 1, 3, 2, 4).reshape(L, D, 2 * DFF)
    pairs = lambda v: v.reshape(*v.shape[:-1], 2, KF, P).swapaxes(-3, -2).reshape(*v.shape[:-1], 2 * DFF)
    down = a["w_down"].reshape(L, 2, DK, P, KD, P).transpose(0, 4, 1, 3, 2, 5)

    def pad(v):
        out = np.zeros((L, P, v.shape[2]), np.float32)
        out[:, :v.shape[1]] = v
        return out

    wide = lambda v: np.broadcast_to(v.reshape(L, 1, -1), (L, P, v.reshape(L, -1).shape[1]))
    chan = lambda v: np.repeat(v.reshape(L, CT, 8, -1), 16, 2).transpose(0, 2, 1, 3).reshape(L, P, -1)
    stat = lambda v: v.reshape(L, ST, P).transpose(0, 2, 1)
    uq = a["mla_w_uq"].reshape(L, 2, QH, HEADS, QK)
    rot = uq[..., NOPE:]
    uqs = np.concatenate([rot[..., ROPE // 2:], rot[..., :ROPE // 2]], -1)
    ukv = a["mla_w_ukv"].reshape(L, P, HEADS, NOPE + HD)
    ls = a["s5_log_step"]
    par = {
        "b_ada": cols(a["b_ada"]), "gm_g": wide(a["gm_ln_g"]), "gm_b": wide(a["gm_ln_b"]),
        "gm_ws": a["gm_ws"].transpose(0, 3, 1, 2).reshape(L, P, -1),
        "gm_bs": np.repeat(a["gm_bs"].reshape(L, CT, 2, P), HD, 2).transpose(0, 2, 1, 3).reshape(L, P, -1),
        "q_norm": pad(a["mla_q_norm"].reshape(L, 2, QH).transpose(0, 2, 1)), "kv_norm": a["mla_kv_norm"][:, :, None],
        "w_uq": pad(uq.transpose(0, 2, 1, 3, 4).reshape(L, QH, -1)),
        "w_uqs": pad(uqs.transpose(0, 2, 1, 3, 4).reshape(L, QH, -1)),
        "w_ukv": np.concatenate([ukv[..., :NOPE].reshape(L, P, -1), ukv[..., NOPE:].reshape(L, P, -1)], 2),
        "s5_are": chan(a["s5_a_re"]), "s5_aim": chan(a["s5_a_im"]),
        "s5_ls": chan(np.repeat(ls[:, :, None], 64, 2)),
        "s5_bre": a["s5_b_re"].transpose(0, 1, 3, 2).reshape(L, CT, P, 64).transpose(0, 2, 1, 3).reshape(L, P, -1),
        "s5_bim": a["s5_b_im"].transpose(0, 1, 3, 2).reshape(L, CT, P, 64).transpose(0, 2, 1, 3).reshape(L, P, -1),
        "s5_cre": a["s5_c_re"].transpose(0, 1, 3, 2).reshape(L, ST, P, 16).transpose(0, 2, 1, 3).reshape(L, P, -1),
        "s5_cim": a["s5_c_im"].transpose(0, 1, 3, 2).reshape(L, ST, P, 16).transpose(0, 2, 1, 3).reshape(L, P, -1),
        "s5_sre": stat(a["s5_a_re"]), "s5_sim": stat(a["s5_a_im"]), "s5_sls": stat(np.repeat(ls[:, :, None], 64, 2)),
        "s5_d": cols(a["s5_d"]), "w_glu": a["s5_w_glu"].reshape(L, CT, P, GW).transpose(0, 2, 1, 3).reshape(L, P, -1),
        "b_glu": cols(a["s5_b_glu"]),
        "hg_lb": np.broadcast_to(a["hg_lb_logits"].reshape(1, L, CT, P).transpose(0, 3, 2, 1), (L, P, CT, L)).reshape(L, P, -1),
        "hg_sel": np.broadcast_to(np.array([[1.0 if 1 <= j <= l else 0.0 for j in range(L)] for l in range(L)],
                                           np.float32).reshape(L, 1, 1, L), (L, P, CT, L)).reshape(L, P, -1),
        "hg_g": cols(a["hg_norm_g"]), "merge": cols(a["merge_g"]), "ln1_g": cols(a["ln1_g"]), "ln1_b": cols(a["ln1_b"]),
        "conv_w": cols(pairs(a["conv_w"])).transpose(0, 2, 3, 1).reshape(L, P, -1), "conv_b": cols(pairs(a["conv_b"])),
        "ln2_g": cols(a["ln2_g"]), "ln2_b": cols(a["ln2_b"]),
        "ln2_a": np.array([ALPHA] * (L - 1) + [1.0], np.float32).reshape(L, 1, 1) + np.zeros((1, P, 1), np.float32),
    }
    pack = lambda names: np.concatenate([par[n].reshape(L, P, w) for n, w in names], 2)

    p = np.arange(P)
    t = np.arange(T)
    inv = np.float32(1.0) / (np.float32(10000.0) ** (np.arange(0, ROPE, 2, dtype=np.float32) / np.float32(ROPE)))
    ang = (t.astype(np.float32)[None, :] * inv[:, None]).astype(np.float64)
    rc, rs = np.ones((P, T)), np.zeros((P, T))
    rc[NOPE:QK] = np.concatenate([np.cos(ang), np.cos(ang)])
    rs[NOPE:QK] = np.concatenate([-np.sin(ang), np.sin(ang)])
    head = np.stack([p // 64 == g for g in range(2)], 1).astype(float)
    const = {
        "rope_c": rc, "rope_s": rs, "iota": np.tile(t, (P, 1)), "reset": np.tile(t % CHUNK != 0, (P, 1)),
        "ident": np.eye(P), "ones": np.ones((P, P)), "head": head, "nhead": 0.0 - head,
        "pair": np.stack([(p // 16) % 2 == g for g in range(2)], 1), "half_pi": np.full((P, 1), 1.5707963),
        "mask_q": np.tile(p < CHUNK, (P, 1)), "mask_k": np.tile(np.where(p >= CHUNK, NEG, 0.0), (P, 1)),
    }
    s_, t_ = p[:, None], p[None, :]
    const["levels"] = np.stack([(s_ // (2 * w) == t_ // (2 * w)) & (s_ % (2 * w) < w) & (t_ % (2 * w) >= w)
                                for w in LEVELS] + [s_ == t_], 1)
    const = {k: v.astype(np.float32) for k, v in const.items()}
    const.update(c=cols(a["c"][0]), lng=cols(a["ln_in_g"]), lnb=cols(a["ln_in_b"]))
    consts = np.concatenate([const[n].reshape(P, w) for n, w in CF], 1)

    arrays = {
        "x": np.swapaxes(a["x"][0].T.reshape(KD, P, T), 0, 1), "consts": consts,
        "par_a": pack(PA), "par_b": pack(PB), "w_ada": chunks(a["w_ada"]), "w_in": chunks(win),
        "w_out": chunks(a["w_out"]), "w_up": chunks(up), "w_down": down.reshape(L, 2 * KD, P, DK, P),
    }
    nc = _bacc.Bacc("TRN2", target_bir_lowering=False, num_devices=1)
    args = []
    for n, v in arrays.items():
        v = np.ascontiguousarray(v)
        if v.ndim == 5:
            v = v.reshape(*v.shape[:3], -1)
        arrays[n] = v
        args.append(nc.dram_tensor(f"in_{n}", v.shape, mybir.dt.from_np(v.dtype), kind="ExternalInput").ap())
    args.append(nc.dram_tensor("out_0", (P, KD, T), F32, kind="ExternalOutput").ap())
    trunk(nc, *args)
    r = _run(nc, [{f"in_{n}": v for n, v in arrays.items()}], core_ids=[0])
    got = r.results[0]["out_0"]
    return np.swapaxes(got, 0, 1).reshape(1, D, T).swapaxes(1, 2)
```

```python
from contextlib import ExitStack

import concourse.bass as bass
from concourse import mybir

F32 = mybir.dt.float32
F32R = mybir.dt.float32r
I32 = mybir.dt.int32
ALU = mybir.AluOpType
ACT = mybir.ActivationFunctionType
AX_X = mybir.AxisListType.X

P = 128
D = 1024
T = 512
L = 2
KD = D // P
NB = T // P
CHUNK = 64
NCH = T // CHUNK
GW = 256
CT = GW // P
QR = 192
QH = QR // 2
ROPE = 32
NOPE = 64
QK = NOPE + ROPE
HEADS = 4
HD = 64
ST = 8
DFF = 2816
KF = DFF // P
NP2 = KF // 2
ALPHA = (2 * L) ** 0.25
SCALE = float(QK) ** -0.5
LEVELS = [32, 16, 8, 4, 2, 1]
NEG = -1.0e30
MAGIC = 12582912.0
TWO_PI = 6.283185

(U0, U1, F0, F1, Q0, Q1, I0, I1, G0, G1, CKV, CQ0, CQ1, AV0, AV1, AU0, AU1) = range(17)
NPROJ = 17
ORDER = [("win", j) for j in range(NPROJ)] + [("out", m) for m in range(KD)] + \
    [("up", m) for m in range(2 * KF)] + [("down", k) for k in range(KF)]
POS = {c: n for n, c in enumerate(ORDER)}
RING = 4
AHEAD = RING - 1
SLOT = KD * P
NCHUNK = len(ORDER)
NVIRT = -(-NCHUNK // RING) * RING
SLOT_TOTAL = [len(range(s, NCHUNK, RING)) for s in range(RING)]
FIRST_OUT, FIRST_UP, FIRST_DOWN = POS[("out", 0)], POS[("up", 0)], POS[("down", 0)]
NSPLIT = NCHUNK - FIRST_OUT
SCRATCH = 24064

MOD_L = 48
MOD_PRE = MOD_BODY = L * MOD_L // (L + 1)
MOD_EARLY = 8
ARING = 2
assert MOD_PRE * (L + 1) == L * MOD_L and MOD_PRE % ARING == 0


DOWN_DONE = [KD - 1] + list(range(KD - 1))


def mods_after(j):
    if j < MOD_EARLY // 2:
        return range(2 * j, 2 * j + 2)
    if 5 <= j < 5 + ST:
        return range(MOD_EARLY + 3 * (j - 5), MOD_EARLY + 3 * (j - 4))
    return range(0)


PA = [("gm_g", GW), ("gm_b", GW), ("gm_ws", HEADS * P), ("gm_bs", CT * P),
      ("q_norm", 2), ("kv_norm", 1), ("w_uq", 2 * HEADS * QK), ("w_uqs", 2 * HEADS * ROPE), ("w_ukv", 2 * GW),
      ("s5_are", CT * 64), ("s5_aim", CT * 64), ("s5_ls", CT * 64), ("s5_bre", CT * 64), ("s5_bim", CT * 64),
      ("s5_cre", ST * 16), ("s5_cim", ST * 16), ("s5_sre", ST), ("s5_sim", ST), ("s5_sls", ST),
      ("s5_d", CT), ("w_glu", CT * GW), ("b_glu", CT), ("hg_lb", CT * L), ("hg_sel", CT * L), ("hg_g", CT),
      ("merge", KD), ("ln1_g", KD), ("ln1_b", KD)]
PB = [("conv_w", 3 * 2 * KF), ("conv_b", 2 * KF), ("ln2_g", KD), ("ln2_b", KD), ("ln2_a", 1)]
CF = [("b_ada", L * MOD_L), ("rope_c", T), ("rope_s", T), ("iota", T), ("reset", T), ("ident", P), ("ones", P),
      ("head", 2), ("nhead", 2),
      ("pair", 2), ("half_pi", 1), ("mask_q", P), ("mask_k", P), ("levels", 7 * P), ("lng", KD), ("lnb", KD)]


def offsets(pack):
    at, o = {}, 0
    for name, n in pack:
        at[name] = (o, n)
        o += n
    return at, o


PA_AT, PA_N = offsets(PA)
PB_AT, PB_N = offsets(PB)
CF_AT, CF_N = offsets(CF)


def trunk(nc, x, consts, c_row, par_a, par_b, w_ada, w_in, w_out, w_up, w_down, out):
    ctx = ExitStack()
    with ctx:
        def sb(name, shape, dt=F32):
            return ctx.enter_context(nc.sbuf_tensor(name, shape, dt))

        banks = [ctx.enter_context(nc.psum_tensor(f"bank{i}", [P, T], F32)) for i in range(8)]

        def twins(name, shape):
            with nc.sbuf_tensor(name, shape, F32) as plain:
                pass
            return plain, sb(name + "_r", shape, F32R)

        xa = sb("xa", [P, KD, T])
        hm, hm_r = twins("hm", [P, KD, T])
        ym, ym_r = twins("ym", [P, KD, T])
        ring, ring_r = twins("ring", [P, RING, SLOT])
        ada = sb("ada", [P, ARING, D])
        silu_c = sb("silu_c", [P, D])
        mods = sb("mods", [P, L * MOD_L])
        pa = sb("pa", [P, PA_N])
        pb = sb("pb", [P, PB_N])
        cf = sb("cf", [P, CF_N])
        mod = sb("mod", [P, 40])
        s1c = sb("s1c", [P, KD])
        s2c = sb("s2c", [P, KD])
        g1p = sb("g1p", [P, KD])
        g2p = sb("g2p", [P, KD])
        ga = sb("ga", [P, 2, KD])
        st = sb("st", [P, 64])
        small = sb("small", [P, 96])
        scr, scr_r = twins("scr", [P, SCRATCH])

        idle = sb("idle", [P, 128])

        taken = [0]

        def carve(n, at=None):
            a = taken[0] if at is None else at
            if at is None:
                taken[0] += n
            assert a + n <= SCRATCH, a + n
            return scr[:, a:a + n]

        def tiles(ap, n, w=T):
            return ap.rearrange("p (n w) -> p n w", w=w)

        sg = tiles(carve(CT * T), CT)
        qt = tiles(carve(CT * T), CT)
        vtok = tiles(carve(NB * GW), NB, GW)
        ckv = tiles(carve(T), 1)
        cq = tiles(carve(2 * T), 2)
        kro = tiles(carve(2 * T), 2)
        avt = tiles(carve(NB * GW), NB, GW)
        tab0 = taken[0]
        cos_t = tiles(carve(ST * T), ST)
        sin_t = tiles(carve(ST * T), ST)
        tab1 = taken[0]
        att = tiles(carve(HEADS * T, tab0), HEADS)
        sbd = tiles(carve(CT * NCH * P, tab0 + HEADS * T), CT * NCH, P)
        ketok = tiles(carve(CT * T, tab0 + HEADS * T + CT * NCH * P), CT)
        ee = tiles(carve(4 * T, tab0 + HEADS * T + CT * NCH * P + CT * T), 4)
        qh = tiles(carve(HEADS * T, tab0), HEADS)
        kt = tiles(carve(HEADS * T, tab0 + HEADS * T), HEADS)
        vb = tiles(carve(NB * GW, tab0 + 2 * HEADS * T), NB, GW)
        ptt = tiles(carve(2 * T, tab0 + 2 * HEADS * T + NB * GW), 2)
        assert tab0 + HEADS * T + CT * NCH * P + CT * T + 4 * T <= tab1
        s50 = taken[0]
        pin = tiles(carve(4 * T), 4)
        bp = tiles(carve(2 * T), 2)
        gg = tiles(carve(2 * T), 2)
        pout = tiles(carve(4 * T), 4)
        hh = tiles(carve(2 * T), 2)
        kc = tiles(carve(CT * T, s50), CT)
        bc = tiles(carve(CT * T, s50 + CT * T), CT)
        ke = tiles(carve(CT * T, s50 + 2 * CT * T), CT)
        qe = tiles(carve(CT * T, s50 + 3 * CT * T), CT)
        pp = tiles(carve(3 * T, s50 + 8 * T), 3)
        qk2 = tiles(carve(4 * T, s50 + 10 * T), 4)
        bd = carve(2 * CT * P).rearrange("p (r c n) -> p r c n", r=2, n=P)
        cbd = carve(2 * ST * 32).rearrange("p (r s n) -> p r s n", r=2, n=32)
        sp_ = carve(12 * P, s50 + 6 * T)
        dg = tiles(carve(2 * T), 2)
        yh = tiles(scr_r[:, 0:KD * T], KD)
        wh0 = KF * T
        wh = tiles(scr_r[:, wh0:wh0 + RING * SLOT], RING, SLOT)
        hf = tiles(carve(KF * T, 0), KF)
        cv0 = wh0 + RING * SLOT
        cv = tiles(carve(6 * T, cv0), 6)
        hs0 = cv0 + 6 * T
        hs = tiles(scr_r[:, hs0:hs0 + 4 * T], 4)
        assert hs0 + 4 * T <= taken[0] - 2 * T and taken[0] == SCRATCH

        early = [ring[:, i, :] for i in range(RING)]
        early += [ym[:, 2 * i:2 * i + 2, :].rearrange("p a t -> p (a t)") for i in range(KD // 2)]
        early += [scr[:, i * D:(i + 1) * D] for i in range((SCRATCH - 2 * T) // D)]
        early += [ada[:, i, :] for i in range(ARING)]
        assert len(early) >= MOD_PRE and SLOT == D
        early = early[-MOD_PRE:]
        early_in = [ctx.enter_context(nc.semaphore(f"early_in{i}")) for i in range(len(early))]

        def sems(*names):
            return {n: ctx.enter_context(nc.semaphore(n)) for n in names}

        ada_in = [ctx.enter_context(nc.semaphore(f"ada_in{i}")) for i in range(ARING)]
        landed = [ctx.enter_context(nc.semaphore(f"landed{i}")) for i in range(RING)]
        S = {
            **sems("const_in", "para_in", "parb_in", "x_in", "chunk_used", "c_in", "layer_done", "mixers_done", "out_done"),
            **sems("dve_chain", "act_chain", "pool_chain"),
            **sems("silu_ready", "ada_used", "mod_ready", "ln_par", "ln_sq", "ln_stat", "ln_var", "ln_sd",
                   "ln_diag", "ln_bcast", "ln_normed", "ln_x", "h_ready", "resid_mm", "resid"),
            **sems("proj_mm", "proj_out"),
            **sems("s5_ang", "s5_trig", "s5_par", "s5_turn", "s5_tab", "s5_b", "s5_pin", "s5_bp", "s5_pout", "s5_h", "s5_c",
                   "s5_y", "s5_gelu", "s5_glu", "s5_gate", "s5_done"),
            **sems("hg_f", "hg_lnf", "hg_b", "hg_arg", "hg_exp", "hg_ke", "hg_ktr", "hg_ktok", "hg_u", "hg_s", "hg_zero",
                   "hg_larg", "hg_lexp", "hg_lqk", "hg_lmm", "hg_lcp", "hg_omm", "hg_osq", "hg_done"),
            **sems("r_sq", "m_sq", "r_stat", "r_var", "r_sd", "r_diag", "r_bcast", "r_used"),
            **sems("q_mm", "q_out", "k_mm", "k_out", "v_mm", "v_out", "sc_mm", "sc_max", "sc_exp", "sc_norm", "pt_mm", "pt_out",
                   "pv_mm", "mla_done"),
            **sems("gm_var", "gm_sd", "gm_vn", "gm_mm", "gm_done"),
            **sems("up_mm", "up_tap", "up_mid", "up_conv", "up_silu", "up_h"),
            **sems("w_hi", "w_lo", "y_out", "y_hi", "y_lo", "h_hi", "h_lo", "f_hi", "f_lo", "down_mm"),
        }

        def p_a(name, a=0, n=None):
            o, w = PA_AT[name]
            return pa[:, o + a:o + (w if n is None else a + n)]

        def p_b(name, a=0, n=None):
            o, w = PB_AT[name]
            return pb[:, o + a:o + (w if n is None else a + n)]

        def c_f(name, a=0, n=None):
            o, w = CF_AT[name]
            return cf[:, o + a:o + (w if n is None else a + n)]

        ident = c_f("ident")
        ones = c_f("ones")
        level_mask = c_f("levels").bitcast(I32).rearrange("p (v t) -> p v t", t=P)
        block = ctx.enter_context(nc.Block())

        sc_banks = [banks[0], banks[1], banks[6]]
        carry = {}
        carried = [0]

        def idle_col():
            carried[0] += 1
            return idle[:, carried[0] - 1:carried[0]]

        def wait_apart(eng, s, value):
            eng.wait_ge(s, value)
            carry[eng]()

        class Chain:

            def __init__(self, eng, s, per_layer):
                self.eng, self.s, self.per, self.l, self.n, self.base = eng, s, per_layer, 0, 0, 0

            def post(self, ins):
                self.n += 1
                ins.then_inc(self.s, 1)
                return ins

            def settle(self):
                self.eng.wait_ge(self.s, self.l * self.per + (self.base + self.n))

            def settle_apart(self):
                wait_apart(self.eng, self.s, self.l * self.per + (self.base + self.n))

            def link(self, ins):
                self.post(ins)
                self.settle()

            def layer(self, l):
                self.base, self.n, self.l = self.base + self.n, 0, l

            def close(self, ins):
                assert self.per > self.n, self.n
                ins.then_inc(self.s, self.per - self.n)

        @block.sync
        def _(sp):
            sp.dma_start(silu_c[:, :], c_row).then_inc(S["c_in"], 16)
            sp.dma_start(cf[:, :], consts).then_inc(S["const_in"], 16)
            for i in range(MOD_PRE):
                sp.dma_start(early[i], w_ada[0, i]).then_inc(early_in[i], 16)
                if i == 1:
                    sp.dma_start(xa[:, :, :], x).then_inc(S["x_in"], 16)
            sp.wait_ge(S["ada_used"], RING)
            with sp.Fori(0, L) as l:
                sp.wait_ge(S["mixers_done"], l + 1)
                sp.dma_start(pa[:, :], par_a[l]).then_inc(S["para_in"], 16)

                def load(n):
                    kind, j = ORDER[n]
                    sp.wait_ge(S["chunk_used"], l * NVIRT + (n + 1))
                    src = {"win": w_in, "out": w_out, "up": w_up, "down": w_down}[kind]
                    sp.dma_start(ring[:, n % RING, :], src[l, j]).then_inc(landed[n % RING], 16)

                for n in range(FIRST_UP):
                    load(n)
                    if n == 4:
                        sp.wait_ge(S["layer_done"], l + 1)
                        sp.dma_start(pb[:, :], par_b[l]).then_inc(S["parb_in"], 16)
                    for i in mods_after(n):
                        sp.wait_ge(S["ada_used"], l * MOD_BODY + (MOD_PRE + i - ARING + 1))
                        sp.dma_start(ada[:, i % ARING, :], w_ada[l + 1, i]).then_inc(ada_in[i % ARING], 16)
                used0 = sp.snap(l * NVIRT + (FIRST_UP + 1))
                with sp.Fori(0, NP2) as i:
                    used = sp.snap(used0 + i * 4)
                    need = [used] + [sp.snap(used + r) for r in range(1, 4)]
                    for r in range(4):
                        n = FIRST_UP + r
                        sp.wait_ge(S["chunk_used"], need[r])
                        sp.dma_start(ring[:, n % RING, :], w_up[l, i * 4 + r]).then_inc(landed[n % RING], 16)
                for n in range(FIRST_DOWN, NCHUNK):
                    load(n)
            sp.wait_ge(S["ln_x"], (2 * L + 1) * KD)
            sp.dma_start(out, xa[:, :, :]).then_inc(S["out_done"], 16)
            sp.wait_ge(S["out_done"], 16)

        @block.tensor
        def _(pe):
            mm = nc.tensor.matmul
            carry[pe] = lambda: mm(banks[7][:, 63:64], ones, ones[:, 0:1], start=True, stop=True)

            def chunk(l, n):
                need = l * (16 * SLOT_TOTAL[n % RING]) + 16 * (n // RING + 1)
                pe.wait_ge(landed[n % RING], need)
                return ring[:, n % RING, :].rearrange("p (k m) -> p k m", m=P)

            def parts(n):
                return [a[:, n % RING, :].rearrange("p (k m) -> p k m", m=P) for a in (wh, ring_r)]

            def thrice(dst, w_hi, w_lo, x_hi, x_lo, start, stop):
                first = mm(dst, w_hi, x_hi, start=start, stop=False)
                mm(dst, w_lo, x_hi, start=False, stop=False)
                return first, mm(dst, w_hi, x_lo, start=False, stop=stop)

            def row_stats(src, nk, rows, col, rhs):
                w = rhs.shape[-1]
                for b in range(NB):
                    for k in range(nk):
                        last = mm(banks[7][:, col + w * b:col + w * (b + 1)], src[0:rows, k, b * P:(b + 1) * P],
                                  rhs, start=(k == 0), stop=(k == nk - 1))
                return last

            def norm_stats(before, n, k):
                pe.wait_ge(S["ln_sq"], before * KD + (n + 1))
                for src, col in ((xa, 64), (hm, 68)):
                    for b in range(NB):
                        last = mm(banks[7][:, col + b:col + b + 1], src[:, k, b * P:(b + 1) * P], ones[:, 0:1],
                                  start=(n == 0 and col + b == 64), stop=(n == KD - 1), skip_group_check=True)
                if n == KD - 1:
                    last.then_inc(S["ln_stat"], 1)

            def norm_spread(n):
                for r in range(2):
                    pe.wait_ge(S["ln_diag"], (n - 1) * 2 + (r + 1))
                    mm(banks[r][:, :], ones, dg[:, r, :], start=True, stop=True).then_inc(S["ln_bcast"], 1)

            pe.wait_ge(S["const_in"], 16)
            mm(banks[7][:, 63:64], ones, ones[:, 0:1], start=True, stop=True).then_inc(S["chunk_used"], RING - 1)
            for k in range(KD):
                norm_stats(0, k, k)
            norm_spread(1)
            with pe.Fori(0, L) as l:
                for k in range(KD):
                    pe.wait_ge(S["h_ready"], (2 * l) * KD + (k + 1))
                def s5_b(t):
                    if t == 0:
                        pe.wait_ge(S["s5_par"], 1 + l)
                        pe.wait_ge(S["proj_out"], l * NPROJ + U1 + 1)
                    else:
                        pe.wait_ge(S["s5_pin"], l * ST + t)
                    c, q = t // 4, t % 4
                    rows = slice(32 * q, 32 * q + 32)
                    for r in range(2):
                        last = mm(banks[2 + r][:, :], bd[rows, r, c, :], ym[rows, 4 + c, :], start=True, stop=True,
                                  tile_position=(32 * q, 0))
                    last.then_inc(S["s5_b"], 1)

                def s5_c(t):
                    pe.wait_ge(S["s5_h"], l * ST + (t + 1))
                    c, q = t // 4, t % 4
                    rows = slice(32 * q, 32 * q + 32)
                    for r in range(2):
                        last = mm(banks[4 + c][rows, :], cbd[:, r, t, :], hh[:, r, :], start=(r == 0), stop=(r == 1))
                    last.then_inc(S["s5_c"], 1)

                for j in range(NPROJ):
                    w = chunk(l, POS[("win", j)])
                    if j >= 2:
                        pe.wait_ge(S["proj_out"], l * NPROJ + j - 1)
                    bank = banks[j % 2]
                    if j in (I0, I1, AV0, AV1):
                        for b in range(NB):
                            for k in range(KD):
                                last = mm(bank[:, b * P:(b + 1) * P], hm[:, k, b * P:(b + 1) * P], w[:, k, :],
                                          start=(k == 0), stop=(k == KD - 1))
                                if b == 0 and k == 0:
                                    last.then_inc(S["chunk_used"], 1)
                    else:
                        for k in range(KD):
                            last = mm(bank[:, :], w[:, k, :], hm[:, k, :], start=(k == 0), stop=(k == KD - 1))
                            if k == 0:
                                last.then_inc(S["chunk_used"], 1)
                    last.then_inc(S["proj_mm"], 1)
                    if 3 <= j < 3 + ST:
                        s5_b(j - 3)
                    if 6 <= j < 6 + ST:
                        s5_c(j - 6)

                pe.wait_ge(S["s5_gelu"], l * CT + CT)
                pe.wait_ge(S["proj_out"], l * NPROJ + NPROJ)
                wg = p_a("w_glu").rearrange("p (k n) -> p k n", n=GW)
                for m in range(CT):
                    for k in range(CT):
                        last = mm(banks[m][:, :], wg[:, k, m * P:(m + 1) * P], ym[:, 4 + k, :], start=(k == 0),
                                  stop=(k == CT - 1))
                last.then_inc(S["s5_glu"], 1)

                pe.wait_ge(S["hg_ke"], l + 1)
                for c in range(CT):
                    for b in range(NB):
                        last = nc.tensor.transpose(banks[2 + c][:, b * P:(b + 1) * P], ke[:, c, b * P:(b + 1) * P], ident)
                last.then_inc(S["hg_ktr"], 1)
                pe.wait_ge(S["hg_ktok"], l + 1)
                pe.wait_ge(S["s5_y"], l * CT + CT)
                for c in range(CT):
                    if c:
                        pe.wait_ge(S["hg_s"], l * CT + 1)
                    for par in range(2):
                        rows = slice(64 * par, 64 * par + 64)
                        for b in range(NB):
                            last = mm(banks[4 + par][:, b * P:(b + 1) * P], ketok[rows, c, b * P:(b + 1) * P],
                                      vtok[rows, b, c * P:(c + 1) * P], start=True, stop=True)
                    last.then_inc(S["hg_u"], 1)
                step = 0
                for lv in range(len(LEVELS) + 1):
                    for c in range(CT):
                        if lv < len(LEVELS):
                            pe.wait_ge(S["hg_lqk"], l * (2 * len(LEVELS)) + step + 1)
                        if step == 0:
                            pe.wait_ge(S["s5_gate"], l + 1)
                        if step >= 2:
                            pe.wait_ge(S["hg_lcp"], l * 14 + step - 1)
                        for hp in range(2):
                            rows = slice(64 * hp, 64 * hp + 64)
                            for b in range(NB):
                                cols = slice(b * P, (b + 1) * P)
                                left = qk2[rows, 2 * (lv % 2) + c, cols] if lv < len(LEVELS) else kc[rows, c, cols]
                                right = qk2[rows, 2 * (lv % 2) + c, cols] if lv < len(LEVELS) else qt[rows, c, cols]
                                last = mm(banks[2 * (step % 2) + hp][:, cols], left, right, start=True, stop=True)
                        last.then_inc(S["hg_lmm"], 1)
                        step += 1
                pe.wait_ge(S["hg_lcp"], l * 14 + 14)
                pe.wait_ge(S["hg_s"], l * CT + CT)
                for c in range(CT):
                    for n in range(1, NCH):
                        mm(banks[4 + c][:, n * 64:(n + 1) * 64], sbd[:, c * NCH + n, :], qe[:, c, n * 64:(n + 1) * 64],
                           start=(n == 1), stop=False, skip_group_check=True)
                    for hp in range(2):
                        for b in range(NB):
                            h = 2 * c + hp
                            last = mm(banks[4 + c][64 * hp:64 * hp + 64, b * P:(b + 1) * P],
                                      vtok[:, b, h * HD:(h + 1) * HD], att[:, h, b * P:(b + 1) * P],
                                      start=False, stop=True, skip_group_check=True)
                last.then_inc(S["hg_omm"], 1)
                pe.wait_ge(S["hg_osq"], l + 1)
                for c in range(CT):
                    last = row_stats(ke[:, c:c + 1, :], 1, P, 80 + 2 * NB * c, c_f("head"))
                last.then_inc(S["r_stat"], 1)
                pe.wait_ge(S["gm_vn"], l + 1)
                wsT = p_a("gm_ws").rearrange("p (h i) -> p h i", i=P)
                for c in range(CT):
                    for hp in range(2):
                        for b in range(NB):
                            h = 2 * c + hp
                            last = mm(banks[2 + c][64 * hp:64 * hp + 64, b * P:(b + 1) * P],
                                      avt[:, b, h * HD:(h + 1) * HD], wsT[:, h, :], start=True, stop=True)
                last.then_inc(S["gm_mm"], 1)

                pe.wait_ge(S["r_diag"], l * 7 + 1)
                for h in range(2):
                    mm(banks[h // 2][64 * (h % 2):64 * (h % 2) + 64, :], ones[:, 0:64], dg[:, h, :], start=True, stop=True)\
                        .then_inc(S["r_bcast"], 1)
                pe.wait_ge(S["r_diag"], l * 7 + 2)
                for h in range(2, 4):
                    mm(banks[h // 2][64 * (h % 2):64 * (h % 2) + 64, :], ones[:, 0:64], dg[:, h - 2, :], start=True,
                       stop=True).then_inc(S["r_bcast"], 1)

                pe.wait_ge(S["r_sq"], l * 2 + 1)
                row_stats(ke, 2, QH, 72, ones[0:QH, 0:1])
                row_stats(qe[:, 0:1, :], 1, P, 76, ones[:, 0:1]).then_inc(S["r_stat"], 1)
                pe.wait_ge(S["r_diag"], l * 7 + 3)
                for r in range(2):
                    last = mm(banks[2 + r][:, :], ones, dg[:, r, :], start=True, stop=True)
                last.then_inc(S["r_bcast"], 1)
                pe.wait_ge(S["r_used"], l + 1)
                for n, g in enumerate((2, 3, 0)):
                    pe.wait_ge(S["m_sq"], l * 6 + (2 * n + 2))
                    row_stats(hm[:, 2 * g:2 * g + 2, :], 2, P, 96 + NB * g, ones[:, 0:1])
                pe.wait_ge(S["r_used"], l + 1)
                wq = p_a("w_uq").rearrange("p (k h m) -> p k h m", k=2, m=QK)
                ws = p_a("w_uqs").rearrange("p (k h m) -> p k h m", k=2, m=ROPE)
                for h in range(HEADS):
                    if h == 0:
                        pe.wait_ge(S["hg_done"], l + 1)
                    if h >= 2:
                        pe.wait_ge(S["q_out"], l * HEADS + h - 1)
                    for k in range(2):
                        mm(banks[2 * (h % 2)][0:QK, :], wq[0:QH, k, h, :], cq[0:QH, k, :], start=(k == 0), stop=(k == 1))
                    for k in range(2):
                        last = mm(banks[2 * (h % 2) + 1][NOPE:QK, :], ws[0:QH, k, h, :], cq[0:QH, k, :],
                                  start=(k == 0), stop=(k == 1))
                    last.then_inc(S["q_mm"], 1)
                wkv = p_a("w_ukv")
                for h in range(HEADS):
                    if h >= 2:
                        pe.wait_ge(S["k_out"], l * HEADS + h - 1)
                    mm(banks[4 + h % 2][0:NOPE, :], wkv[:, h * NOPE:(h + 1) * NOPE], ckv[:, 0, :], start=True, stop=True)\
                        .then_inc(S["k_mm"], 1)
                for b in range(NB):
                    if b == 1:
                        pe.wait_ge(S["k_out"], l * HEADS + HEADS)
                    if b >= 2:
                        pe.wait_ge(S["v_out"], l * NB + b - 1)
                    bank = banks[6] if b % 2 == 0 else banks[4]
                    mm(bank[:, 0:GW], ckv[:, 0, b * P:(b + 1) * P], wkv[:, GW:2 * GW], start=True, stop=True)\
                        .then_inc(S["v_mm"], 1)

                def scores(i):
                    h, b = i // NB, i % NB
                    if i == 0:
                        pe.wait_ge(S["q_out"], l * HEADS + HEADS)
                        pe.wait_ge(S["v_out"], l * NB + NB)
                        pe.wait_ge(S["k_out"], l * HEADS + HEADS)
                    if i >= 3:
                        pe.wait_ge(S["sc_exp"], l * 16 + i - 2)
                    mm(sc_banks[i % 3][:, 0:(b + 1) * P], qh[0:QK, h, b * P:(b + 1) * P], kt[0:QK, h, 0:(b + 1) * P],
                       start=True, stop=False, skip_group_check=True)
                    mm(sc_banks[i % 3][:, b * P:(b + 1) * P], c_f("mask_q")[0:1, :], c_f("mask_k")[0:1, :], start=False,
                       stop=True, skip_group_check=True).then_inc(S["sc_mm"], 1)

                def turn(i):
                    b = i % NB
                    pe.wait_ge(S["sc_norm"], l * 16 + i + 1)
                    if i >= 2:
                        pe.wait_ge(S["pt_out"], l * 16 + i - 1)
                    for k in range(b + 1):
                        last = nc.tensor.transpose(banks[2 + i % 2][:, k * P:(k + 1) * P], pp[:, i % 3, k * P:(k + 1) * P],
                                                   ident)
                    last.then_inc(S["pt_mm"], 1)

                def values(i):
                    h, b = i // NB, i % NB
                    pe.wait_ge(S["pt_out"], l * 16 + i + 1)
                    for k in range(b + 1):
                        last = mm(banks[4 + h // 2][64 * (h % 2):64 * (h % 2) + 64, b * P:(b + 1) * P],
                                  vb[:, k, h * HD:(h + 1) * HD], ptt[:, i % 2, k * P:(k + 1) * P],
                                  start=(k == 0), stop=(k == b))
                    last.then_inc(S["pv_mm"], 1)

                for i in range(16 + 3):
                    if i < 16:
                        scores(i)
                    if 2 <= i < 18:
                        turn(i - 2)
                    if i >= 3:
                        values(i - 3)

                pe.wait_ge(S["r_sq"], l * 2 + 2)
                row_stats(hm[:, 2:4, :], 2, P, 96 + NB, ones[:, 0:1]).then_inc(S["r_stat"], 1)
                for g in range(4):
                    pe.wait_ge(S["r_diag"], l * 7 + 4 + g)
                    mm(banks[g][:, :], ones, dg[:, g % 2, :], start=True, stop=True).then_inc(S["r_bcast"], 1)
                for m in range(KD):
                    w_hi, w_lo = parts(FIRST_OUT + m)
                    pe.wait_ge(S["w_lo"], l * NSPLIT + (m + 1))
                    if m >= 4:
                        pe.wait_ge(S["resid"], (2 * l) * KD + m - 3)
                    for k in range(KD):
                        if m == 0:
                            pe.wait_ge(S["y_lo"], l * KD + (k + 1))
                        first, last = thrice(banks[m % 4][:, :], w_hi[:, k, :], w_lo[:, k, :], yh[:, k, :],
                                             ym_r[:, k, :], k == 0, k == KD - 1)
                        if k == 0:
                            first.then_inc(S["chunk_used"], 1)
                    last.then_inc(S["resid_mm"], 1)
                    if m >= 2:
                        norm_stats(2 * l + 1, m - 2, m - 2)
                for k in range(KD - 2, KD):
                    norm_stats(2 * l + 1, k, k)
                norm_spread(2 * l + 2)

                with pe.Fori(0, NP2) as i:
                    for r in range(4):
                        w_hi, w_lo = parts(FIRST_UP + r)
                        pe.wait_ge(S["w_lo"], l * NSPLIT + i * 4 + (FIRST_UP - FIRST_OUT + r + 1))
                        pe.wait_ge(S["up_conv"], l * (2 * KF) + i * 4 + (r + 1))
                        for k in range(KD):
                            if r == 0:
                                pe.wait_ge(S["h_lo"], l * KD + (k + 1))
                            first, last = thrice(banks[2 + r][:, :], w_hi[:, k, :], w_lo[:, k, :], ym_r[:, k, :],
                                                 hm_r[:, k, :], k == 0, k == KD - 1)
                            if k == 0:
                                first.then_inc(S["chunk_used"], 1)
                        last.then_inc(S["up_mm"], 1)

                def down(k, slot, half, f_need, w_need):
                    pe.wait_ge(S["f_lo"], f_need)
                    pe.wait_ge(S["w_lo"], w_need)
                    w_hi, w_lo = parts(slot)
                    for m in (DOWN_DONE if k == KF - 1 else range(KD)):
                        first, last = thrice(banks[m][:, :], w_hi[:, m, :], w_lo[:, m, :], hs[:, half, :],
                                             hs[:, 2 + half, :], k == 0, k == KF - 1)
                        if m == (KD - 1 if k == KF - 1 else 0):
                            first.then_inc(S["chunk_used"], 1)
                        if k == KF - 1:
                            last.then_inc(S["resid_mm"], 1)
                    if k < KF - 1:
                        last.then_inc(S["down_mm"], 1)

                w_down0 = FIRST_DOWN - FIRST_OUT
                pe.wait_ge(S["up_conv"], l * (2 * KF) + (2 * KF + 4))
                down(0, FIRST_DOWN, 0, l * KF + 1, l * NSPLIT + (w_down0 + 1))
                with pe.Fori(0, KF // 4) as i:
                    for r in range(4):
                        down(1 + r, FIRST_DOWN + 1 + r, (1 + r) % 2, l * KF + i * 4 + (r + 2),
                             l * NSPLIT + i * 4 + (w_down0 + r + 2))
                down(KF - 1, NCHUNK - 1, (KF - 1) % 2, l * KF + KF, l * NSPLIT + NSPLIT)
                pe.wait_ge(S["ln_sq"], (2 * l + 2) * KD + 1)
                mm(banks[7][:, 63:64], ones, ones[:, 0:1], start=True, stop=True).then_inc(S["chunk_used"], NVIRT - NCHUNK)
                for n, k in enumerate(DOWN_DONE):
                    norm_stats(2 * l + 2, n, k)
                norm_spread(2 * l + 3)

        @block.vector
        def _(v):
            V = nc.vector
            carry[v] = lambda: V.memset(idle_col(), 0.0)
            ch = Chain(v, S["dve_chain"], 1024)

            def norm(n):
                v.wait_ge(S["ln_stat"], n)
                mean, sq, var, rstd, mr = (st[:, 4 * i:4 * i + 4] for i in range(5))
                ch.post(V.tensor_scalar(mean, banks[7][:, 64:68], 1.0 / D, None, ALU.mult))
                ch.link(V.tensor_scalar(sq, banks[7][:, 68:72], 1.0 / D, 1e-5, ALU.mult, ALU.add))
                ch.link(V.tensor_tensor(var, mean, mean, ALU.mult))
                ch.link(V.tensor_tensor(var, sq, var, ALU.subtract))
                V.tensor_scalar(var, var, 1e-5, None, ALU.max).then_inc(S["ln_var"], 1)
                v.wait_ge(S["ln_sd"], n)
                ch.link(V.reciprocal(rstd, var))
                ch.post(V.tensor_tensor(mr, mean, rstd, ALU.mult))
                for b in range(NB):
                    ins = V.tensor_scalar(dg[:, 0, b * P:(b + 1) * P], ident, rstd[:, b:b + 1], None, ALU.mult)
                ins.then_inc(S["ln_diag"], 1)
                ch.settle()
                for b in range(NB):
                    ins = V.tensor_scalar(dg[:, 1, b * P:(b + 1) * P], ident, mr[:, b:b + 1], None, ALU.mult)
                ins.then_inc(S["ln_diag"], 1)
                v.wait_ge(S["ln_bcast"], (n - 1) * 2 + 1)
                for k in range(KD + 1):
                    if k < KD:
                        ch.post(V.tensor_tensor(xa[:, k, :], xa[:, k, :], banks[0][:, :], ALU.mult))
                    if k == KD:
                        ch.settle()
                    if k == 1:
                        v.wait_ge(S["ln_bcast"], (n - 1) * 2 + 2)
                    if k:
                        V.tensor_tensor(xa[:, k - 1, :], xa[:, k - 1, :], banks[1][:, :], ALU.subtract)\
                            .then_inc(S["ln_normed"], 1)
                    if k < KD:
                        ch.settle()

            def modulation(f, dst):
                w = early[f]
                v.wait_ge(early_in[f], 16)
                V.scalar_tensor_tensor(w, w, 1.0, silu_c[:, :], ALU.mult, ALU.mult, accum_out=dst).then_inc(S["ada_used"], 1)

            def modulation_body(l, i):
                slot = i % ARING
                v.wait_ge(ada_in[slot], l * (16 * MOD_BODY // ARING) + 16 * (i // ARING + 1))
                V.scalar_tensor_tensor(ada[:, slot, :], ada[:, slot, :], 1.0, silu_c[:, :], ALU.mult, ALU.mult,
                                       accum_out=mods[:, bass.ds(l * MOD_BODY + (MOD_PRE + i), 1)])\
                    .then_inc(S["ada_used"], 1)

            def rows_rstd(n_stat, n_sd, cols, width, inv_n, eps, dst):
                v.wait_ge(S["r_stat"], n_stat)
                V.tensor_scalar(st[:, dst:dst + width], banks[7][:, cols:cols + width], inv_n, eps, ALU.mult, ALU.add)\
                    .then_inc(S["r_var"], 1)
                v.wait_ge(S["r_sd"], n_sd)
                ch.link(V.reciprocal(st[:, dst:dst + width], st[:, dst:dst + width]))

            def diagonals(r, cols, last_inc):
                for b in range(NB):
                    ins = V.tensor_scalar(dg[:, r, b * P:(b + 1) * P], ident, st[:, cols[b]:cols[b] + 1], None, ALU.mult)
                if last_inc:
                    ins.then_inc(S["r_diag"], 1)

            v.wait_ge(S["const_in"], 16)
            V.tensor_scalar(ga[:, :, :], c_f("lng", 0, 2 * KD).rearrange("p (a b) -> p a b", a=2), ALPHA, None, ALU.mult)\
                .then_inc(S["ln_par"], 1)
            V.memset(small[:, 90:91], 0.0).then_inc(S["mixers_done"], 1)
            V.memset(small[:, 91:92], 0.0).then_inc(S["layer_done"], 1)
            v.wait_ge(S["silu_ready"], 1)
            for i in range(MOD_PRE - KD):
                modulation(i, mods[:, i:i + 1])
            norm(1)
            for i in range(MOD_PRE - KD, MOD_PRE):
                modulation(i, mods[:, i:i + 1])
            V.memset(small[:, 88:89], 0.0).then_inc(S["up_conv"], 4)
            V.memset(small[:, 89:90], 0.0).then_inc(S["up_h"], 2)
            with v.Fori(0, L) as l:
                ch.layer(l)
                v.wait_ge(S["ln_x"], (2 * l + 1) * KD)
                v.wait_ge(S["para_in"], 16 * l + 16)
                W = lambda i: sp_[:, i * P:(i + 1) * P]
                are, aim = p_a("s5_are"), p_a("s5_aim")
                v.wait_ge(S["s5_ang"], 3 * l + 1)
                ch.post(V.tensor_tensor(W(1), W(0), are, ALU.mult))
                ch.post(V.tensor_tensor(W(2), W(0), aim, ALU.mult))
                ch.post(V.tensor_tensor(small[:, 0:8], small[:, 24:32], p_a("s5_sre"), ALU.mult))
                ch.post(V.tensor_tensor(small[:, 8:16], small[:, 24:32], p_a("s5_sim"), ALU.mult))
                ch.settle()
                ch.post(V.tensor_scalar(W(2), W(2), 1.0 / 6.283185307179586, None, ALU.mult))
                ch.post(V.tensor_scalar(small[:, 8:16], small[:, 8:16], 1.0 / 6.283185307179586, None, ALU.mult))
                ch.settle()
                ch.link(V.tensor_scalar(W(3), W(2), MAGIC, None, ALU.add))
                ch.link(V.scalar_tensor_tensor(W(3), W(3), MAGIC, W(2), ALU.subtract, ALU.subtract))
                V.scalar_tensor_tensor(W(4), W(3), -1.0, W(3), ALU.mult, ALU.max).then_inc(S["s5_ang"], 1)
                v.wait_ge(S["s5_trig"], l + 1)
                ch.post(V.tensor_tensor(W(6), W(5), W(6), ALU.mult))
                ch.post(V.tensor_tensor(W(7), W(5), W(7), ALU.mult))
                ch.post(V.tensor_tensor(W(8), are, are, ALU.mult))
                ch.post(V.tensor_tensor(W(9), aim, aim, ALU.mult))
                ch.settle()
                ch.post(V.tensor_scalar(W(6), W(6), -1.0, None, ALU.add))
                ch.post(V.tensor_tensor(W(8), W(8), W(9), ALU.add))
                ch.settle()
                ch.post(V.reciprocal(W(8), W(8)))
                ch.post(V.tensor_tensor(W(9), W(6), are, ALU.mult))
                ch.post(V.tensor_tensor(W(10), W(7), aim, ALU.mult))
                ch.post(V.tensor_tensor(W(11), W(7), are, ALU.mult))
                ch.post(V.tensor_tensor(W(0), W(6), aim, ALU.mult))
                ch.settle()
                ch.post(V.tensor_tensor(W(9), W(9), W(10), ALU.add))
                ch.post(V.tensor_tensor(W(11), W(11), W(0), ALU.subtract))
                ch.settle()
                ch.post(V.tensor_tensor(W(9), W(9), W(8), ALU.mult))
                ch.post(V.tensor_tensor(W(11), W(11), W(8), ALU.mult))
                ch.settle()
                ch.post(V.tensor_tensor(W(1), W(9), p_a("s5_bre"), ALU.mult))
                ch.post(V.tensor_tensor(W(2), W(11), p_a("s5_bim"), ALU.mult))
                ch.post(V.tensor_tensor(W(3), W(9), p_a("s5_bim"), ALU.mult))
                ch.post(V.tensor_tensor(W(4), W(11), p_a("s5_bre"), ALU.mult))
                ch.settle()
                ch.post(V.tensor_tensor(W(1), W(1), W(2), ALU.subtract))
                ch.post(V.tensor_tensor(W(3), W(3), W(4), ALU.add))
                ch.settle()
                for r in range(2):
                    src = W(1 + 2 * r).rearrange("p (c n) -> p c n", c=CT)
                    for g in range(2):
                        ch.post(V.tensor_scalar(bd[:, r, :, 64 * g:64 * g + 64], src, c_f("pair", g, 1), None, ALU.mult))
                for r, nm in ((0, "s5_cre"), (1, "s5_cim")):
                    src = p_a(nm).rearrange("p (s n) -> p s n", n=16)
                    hd = "nhead" if r else "head"
                    for g in range(2):
                        ch.post(V.tensor_scalar(cbd[:, r, :, 16 * g:16 * g + 16], src, c_f(hd, g, 1), None, ALU.mult))
                wsT = p_a("gm_ws").rearrange("p (h i) -> p h i", i=P)
                ch.post(V.memset(wsT[64:128, :, 0:64], 0.0))
                lg = p_a("hg_lb").rearrange("p (c j) -> p c j", j=L)
                lb, omlb = small[:, 40:42], small[:, 42:44]
                ch.post(V.tensor_tensor(small[:, 44:46], lg[:, :, 0], lg[:, :, 1], ALU.max))
                ch.settle()
                for j in range(L):
                    ins = V.tensor_tensor(small[:, 46 + 2 * j:48 + 2 * j], lg[:, :, j], small[:, 44:46], ALU.subtract)
                ins.then_inc(S["s5_par"], 1)

                def s5_in(t):
                    v.wait_ge(S["s5_b"], l * ST + t + 1)
                    v.wait_ge(S["s5_tab"], l * ST + t + 1)
                    if t:
                        v.wait_ge(S["s5_bp"], l * ST + t)
                    ch.post(V.tensor_tensor(pin[:, 0, :], banks[2][:, :], cos_t[:, t, :], ALU.mult))
                    ch.post(V.tensor_tensor(pin[:, 1, :], banks[3][:, :], sin_t[:, t, :], ALU.mult))
                    ch.post(V.tensor_tensor(pin[:, 2, :], banks[3][:, :], cos_t[:, t, :], ALU.mult))
                    ch.settle()
                    V.tensor_tensor(pin[:, 3, :], banks[2][:, :], sin_t[:, t, :], ALU.mult).then_inc(S["s5_pin"], 1)

                def s5_out(t):
                    v.wait_ge(S["s5_bp"], l * ST + t + 1)
                    if t:
                        v.wait_ge(S["s5_h"], l * ST + t)
                    mag = small[:, 32 + t:33 + t].to_broadcast([P, T])
                    for r in range(2):
                        ch.post(V.tensor_tensor_scan(gg[:, r, :], mag, bp[:, r, :], 0.0, ALU.mult, ALU.add))
                    ch.settle()
                    ch.post(V.tensor_tensor(pout[:, 0, :], gg[:, 0, :], cos_t[:, t, :], ALU.mult))
                    ch.post(V.tensor_tensor(pout[:, 1, :], gg[:, 1, :], sin_t[:, t, :], ALU.mult))
                    ch.post(V.tensor_tensor(pout[:, 2, :], gg[:, 1, :], cos_t[:, t, :], ALU.mult))
                    ch.settle()
                    V.tensor_tensor(pout[:, 3, :], gg[:, 0, :], sin_t[:, t, :], ALU.mult).then_inc(S["s5_pout"], 1)

                def s5_skip(c):
                    v.wait_ge(S["s5_c"], l * ST + 4 * c + 4)
                    V.scalar_tensor_tensor(ym[:, 4 + c, :], ym[:, 4 + c, :], p_a("s5_d", c, 1), banks[4 + c][:, :],
                                           ALU.mult, ALU.add).then_inc(S["s5_y"], 1)

                for i in range(MOD_EARLY):
                    modulation_body(l, i)
                for t in range(ST + 1):
                    if t < ST:
                        modulation_body(l, MOD_EARLY + 3 * t)
                        s5_in(t)
                        modulation_body(l, MOD_EARLY + 3 * t + 1)
                    if t:
                        s5_out(t - 1)
                    if t < ST:
                        modulation_body(l, MOD_EARLY + 3 * t + 2)
                s5_skip(0)
                s5_skip(1)
                v.wait_ge(S["ada_used"], l * MOD_BODY + (MOD_PRE + MOD_BODY))
                ch.post(V.tensor_tensor(mod[:, 16:40], mods[:, bass.ds(l * MOD_L + 16, 24)],
                                        c_f("b_ada")[:, bass.ds(l * MOD_L + 16, 24)], ALU.add))
                ch.post(V.tensor_tensor(g2p[:, :], mods[:, bass.ds(l * MOD_L + 40, 8)],
                                        c_f("b_ada")[:, bass.ds(l * MOD_L + 40, 8)], ALU.add))
                ch.settle()
                ch.post(V.tensor_scalar(g2p[:, :], g2p[:, :], 1.0, None, ALU.add))
                ch.post(V.tensor_scalar(g1p[:, :], mod[:, 16:24], 1.0, None, ALU.add))
                V.tensor_scalar(s2c[:, :], mod[:, 32:40], 1.0, 1.0 / ALPHA, ALU.add, ALU.mult).then_inc(S["mod_ready"], 1)
                V.tensor_scalar(ga[:, :, :], p_a("ln1_g", 0, 2 * KD).rearrange("p (a b) -> p a b", a=2), ALPHA, None,
                                ALU.mult).then_inc(S["ln_par"], 1)

                v.wait_ge(S["s5_ang"], 3 * l + 3)
                ch.link(V.tensor_tensor(small[:, 50:52], small[:, 46:48], small[:, 48:50], ALU.add))
                ch.link(V.reciprocal(small[:, 50:52], small[:, 50:52]))
                ch.link(V.tensor_tensor(small[:, 52:54], small[:, 48:50], small[:, 50:52], ALU.mult))
                sel = p_a("hg_sel").rearrange("p (c j) -> p c j", j=L)
                ch.link(V.tensor_tensor(lb, small[:, 52:54], sel[:, :, 1], ALU.mult))
                ch.link(V.tensor_scalar(omlb, lb, -1.0, 1.0, ALU.mult, ALU.add))
                v.wait_ge(S["proj_out"], l * NPROJ + F1 + 1)
                for c in range(CT):
                    ch.post(V.tensor_scalar(bc[:, c, :], sg[:, c, :], omlb[:, c:c + 1], lb[:, c:c + 1], ALU.mult, ALU.add))
                ch.settle()
                for c in range(CT):
                    ch.post(V.tensor_scalar(kc[:, c, :], bc[:, c, :], -1.0, 1.0, ALU.mult, ALU.add))
                ch.settle()
                for c in range(CT):
                    ins = V.tensor_scalar(bc[:, c, :], bc[:, c, :], 2.0 ** -63, None, ALU.max)
                    ins.then_inc(S["hg_f"], 1)
                v.wait_ge(S["hg_lnf"], l + 1)
                for c in range(CT):
                    ch.post(V.tensor_tensor_scan(bc[:, c, :], c_f("reset"), sg[:, c, :], 0.0, ALU.mult, ALU.add))
                ch.settle()
                for c in range(CT):
                    b3 = bc[:, c, :].rearrange("p (n t) -> p n t", t=CHUNK)
                    ins = V.tensor_tensor(sg[:, c, :].rearrange("p (n t) -> p n t", t=CHUNK),
                                          b3[:, :, CHUNK - 1:CHUNK].to_broadcast([P, NCH, CHUNK]), b3, ALU.subtract)
                    ins.then_inc(S["hg_arg"], 1)
                v.wait_ge(S["hg_exp"], l + 1)
                dec = small[:, 56:72].rearrange("p (c n) -> p c n", c=CT)
                for c in range(CT):
                    ch.post(V.tensor_copy(dec[:, c, :], qe[:, c, :].rearrange("p (n t) -> p n t", t=CHUNK)[:, :, CHUNK - 1]))
                ch.post(V.tensor_tensor(ke[:, 0, :], ke[:, 0, :], kc[:, 0, :], ALU.mult))
                ch.settle()
                V.tensor_tensor(ke[:, 1, :], ke[:, 1, :], kc[:, 1, :], ALU.mult).then_inc(S["hg_ke"], 1)
                v.wait_ge(S["proj_out"], l * NPROJ + Q1 + 1)
                for c in range(CT):
                    ch.post(V.tensor_tensor(qe[:, c, :], qe[:, c, :], qt[:, c, :], ALU.mult))
                v.wait_ge(S["s5_gate"], l + 1)
                for c in range(CT):
                    ins = V.tensor_tensor(ym[:, 4 + c, :], ym[:, 4 + c, :], pout[:, c, :], ALU.mult)
                    ins.then_inc(S["s5_done"], 1)
                def level_exponents(lv):
                    w = LEVELS[lv]
                    for c in range(CT):
                        if lv >= 2:
                            v.wait_ge(S["hg_lqk"], l * 12 + 2 * (lv - 2) + c + 1)
                        b4 = bc[:, c, :].rearrange("p (n t) -> p n t", t=2 * w)
                        e4 = ee[:, 2 * (lv % 2) + c, :].rearrange("p (n t) -> p n t", t=2 * w)
                        ref = b4[:, :, w - 1:w].to_broadcast([P, T // (2 * w), w])
                        ch.post(V.tensor_tensor(e4[:, :, 0:w], ref, b4[:, :, 0:w], ALU.subtract))
                        ch.settle()
                        V.tensor_tensor(e4[:, :, w:2 * w], b4[:, :, w:2 * w], ref, ALU.subtract).then_inc(S["hg_larg"], 1)

                level_exponents(0)
                level_exponents(1)

                v.wait_ge(S["hg_zero"], l + 1)
                for c in range(CT):
                    v.wait_ge(S["hg_u"], l * CT + c + 1)
                    for n in range(1, NCH):
                        src_bank = banks[4 + (n - 1) % 2]
                        b = (n - 1) // 2
                        for hp in range(2):
                            r = slice(64 * hp, 64 * hp + 64)
                            new = sbd[r, c * NCH + n, 64 * hp:64 * hp + 64]
                            add = src_bank[r, b * P + 64 * hp:b * P + 64 * hp + 64]
                            if n == 1:
                                ins = V.tensor_copy(new, add)
                            else:
                                ins = V.scalar_tensor_tensor(new, sbd[r, c * NCH + n - 1, 64 * hp:64 * hp + 64],
                                                             dec[r, c, n - 1:n], add, ALU.mult, ALU.add)
                        if n < NCH - 1:
                            ch.link(ins)
                    ins.then_inc(S["hg_s"], 1)

                def level_operands(lv):
                    w = LEVELS[lv]
                    for c in range(CT):
                        e4 = ee[:, 2 * (lv % 2) + c, :].rearrange("p (n t) -> p n t", t=2 * w)
                        q4 = qk2[:, 2 * (lv % 2) + c, :].rearrange("p (n t) -> p n t", t=2 * w)
                        v.wait_ge(S["hg_lexp"], l * 12 + 2 * lv + c + 1)
                        if lv >= 2:
                            v.wait_ge(S["hg_lmm"], l * 14 + 2 * (lv - 2) + c + 1)
                        ch.post(V.tensor_tensor(q4[:, :, 0:w], e4[:, :, 0:w],
                                                kc[:, c, :].rearrange("p (n t) -> p n t", t=2 * w)[:, :, 0:w], ALU.mult))
                        ch.settle()
                        V.tensor_tensor(q4[:, :, w:2 * w], e4[:, :, w:2 * w],
                                        qt[:, c, :].rearrange("p (n t) -> p n t", t=2 * w)[:, :, w:2 * w],
                                        ALU.mult).then_inc(S["hg_lqk"], 1)

                def level_take(lv):
                    for c in range(CT):
                        step = 2 * lv + c
                        wait_apart(v, S["hg_lmm"], l * 14 + step + 1)
                        for hp in range(2):
                            a3 = att[:, 2 * c + hp, :].rearrange("p (b t) -> p b t", t=P)
                            ins = V.copy_predicated(a3, level_mask[:, lv:lv + 1, :].to_broadcast([P, NB, P]),
                                                    banks[2 * (step % 2) + hp][:, :].rearrange("p (b t) -> p b t", t=P))
                        ins.then_inc(S["hg_lcp"], 1)

                for lv in range(len(LEVELS) + 1):
                    if 1 < lv + 1 < len(LEVELS):
                        level_exponents(lv + 1)
                    if lv < len(LEVELS):
                        level_operands(lv)
                    if lv:
                        level_take(lv - 1)
                level_take(len(LEVELS))
                v.wait_ge(S["proj_out"], l * NPROJ + AV1 + 1)
                bn = small[:, 0:24].rearrange("p (b s) -> p b s", b=NB)
                ag = small[:, 24:32].rearrange("p (b s) -> p b s", b=NB)
                v.wait_ge(S["s5_h"], l * ST + ST)
                for b in range(NB):
                    ch.post(V.bn_stats(bn[:, b, :], avt[:, b, :]))
                ch.settle_apart()
                for b in range(NB):
                    ch.post(V.bn_aggr(ag[:, b, :], bn[:, b, :]))
                ch.settle()
                V.tensor_scalar(st[:, 56:60], ag[:, :, 1], 1e-5, None, ALU.add).then_inc(S["gm_var"], 1)
                v.wait_ge(S["gm_sd"], l + 1)
                ch.link(V.reciprocal(st[:, 56:60], st[:, 56:60]))
                for b in range(NB):
                    ch.post(V.tensor_scalar(avt[:, b, :], avt[:, b, :], ag[:, b, 0:1], st[:, 56 + b:57 + b], ALU.subtract,
                                            ALU.mult))
                ch.settle()
                for b in range(NB):
                    ch.post(V.tensor_tensor(avt[:, b, :], avt[:, b, :], p_a("gm_g"), ALU.mult))
                ch.settle()
                for b in range(NB):
                    ins = V.tensor_tensor(avt[:, b, :], avt[:, b, :], p_a("gm_b"), ALU.add)
                ins.then_inc(S["gm_vn"], 1)
                rows_rstd(l * 3 + 1, l * 3 + 1, 80, 16, 1.0 / HD, 1e-6, 24)
                for c in range(CT):
                    for hp in range(2):
                        diagonals(hp, [24 + 8 * c + 2 * b + hp for b in range(NB)], hp == 1)
                    v.wait_ge(S["r_bcast"], l * 9 + 2 * c + 2)
                for c in range(CT):
                    ch.post(V.scalar_tensor_tensor(ym[:, 6 + c, :], ym[:, 6 + c, :], p_a("hg_g", c, 1), banks[c][:, :],
                                                   ALU.mult, ALU.mult))
                ch.settle()
                ch.post(V.tensor_tensor(ym[:, 6, :], ym[:, 6, :], banks[4][:, :], ALU.mult))
                ch.settle()
                V.tensor_tensor(ym[:, 7, :], ym[:, 7, :], banks[5][:, :], ALU.mult).then_inc(S["hg_done"], 1)

                v.wait_ge(S["gm_mm"], l + 1)
                for c in range(CT):
                    for b in range(NB):
                        cols = slice(b * P, (b + 1) * P)
                        ch.post(V.tensor_tensor(kc[:, c, cols], banks[2 + c][:, cols], p_a("gm_bs", c * P, P), ALU.add))
                ch.settle()
                v.wait_ge(S["proj_out"], l * NPROJ + NPROJ)
                for c in range(CT):
                    ins = V.tensor_tensor(ym[:, c, :], ym[:, c, :], kc[:, c, :], ALU.mult)
                    ins.then_inc(S["gm_done"], 1)

                v.wait_ge(S["r_stat"], l * 3 + 2)
                ch.post(V.tensor_scalar(st[:, 40:44], banks[7][:, 72:76], 1.0 / QR, 1e-6, ALU.mult, ALU.add))
                ch.settle()
                V.tensor_scalar(st[:, 44:48], banks[7][:, 76:80], 1.0 / P, 1e-6, ALU.mult, ALU.add).then_inc(S["r_var"], 1)
                v.wait_ge(S["r_sd"], l * 3 + 2)
                ch.link(V.reciprocal(st[:, 40:48], st[:, 40:48]))
                diagonals(0, [40, 41, 42, 43], False)
                diagonals(1, [44, 45, 46, 47], True)
                v.wait_ge(S["r_bcast"], l * 9 + 5)
                for k in range(2):
                    ch.post(V.scalar_tensor_tensor(cq[0:QH, k, :], cq[0:QH, k, :], p_a("q_norm", k, 1)[0:QH, :],
                                                   banks[2][0:QH, :], ALU.mult, ALU.mult))
                ch.settle()
                V.scalar_tensor_tensor(ckv[:, 0, :], ckv[:, 0, :], p_a("kv_norm"), banks[3][:, :], ALU.mult, ALU.mult)\
                    .then_inc(S["r_used"], 1)
                kk, ks = kro[NOPE:QK, 0, :], kro[NOPE:QK, 1, :]
                ch.post(V.tensor_tensor(kk, kk, c_f("rope_c")[NOPE:QK, :], ALU.mult))
                ch.post(V.tensor_tensor(ks, ks, c_f("rope_s")[NOPE:QK, :], ALU.mult))
                ch.settle()
                for h in range(HEADS):
                    ch.post(V.tensor_tensor(kt[NOPE:QK, h, :], kk, ks, ALU.add))
                for h in range(HEADS):
                    v.wait_ge(S["q_mm"], l * HEADS + h + 1)
                    ch.post(V.tensor_tensor(qh[0:QK, h, :], banks[2 * (h % 2)][0:QK, :], c_f("rope_c")[0:QK, :], ALU.mult))
                    ch.post(V.tensor_tensor(ptt[NOPE:QK, h % 2, :], banks[2 * (h % 2) + 1][NOPE:QK, :],
                                            c_f("rope_s")[NOPE:QK, :], ALU.mult))
                    ch.settle()
                    V.tensor_tensor(qh[NOPE:QK, h, :], qh[NOPE:QK, h, :], ptt[NOPE:QK, h % 2, :], ALU.add)\
                        .then_inc(S["q_out"], 1)

                row_max, neg_max, row_sum, inv_sum = (small[:, 72 + 3 * q:75 + 3 * q] for q in range(4))

                def softmax_max(i):
                    b, q = i % NB, i % 3
                    v.wait_ge(S["sc_mm"], l * 16 + i + 1)
                    ch.link(V.tensor_reduce(row_max[:, q:q + 1], sc_banks[q][:, 0:(b + 1) * P], AX_X, ALU.max))
                    if i >= 3:
                        v.wait_ge(S["sc_exp"], l * 16 + i - 2)
                    V.tensor_scalar(neg_max[:, q:q + 1], row_max[:, q:q + 1], -SCALE, None, ALU.mult)\
                        .then_inc(S["sc_max"], 1)

                def softmax_norm(i):
                    b, q = i % NB, i % 3
                    v.wait_ge(S["sc_exp"], l * 16 + i + 1)
                    ch.link(V.reciprocal(inv_sum[:, q:q + 1], row_sum[:, q:q + 1]))
                    V.tensor_scalar(pp[:, q, 0:(b + 1) * P], pp[:, q, 0:(b + 1) * P], inv_sum[:, q:q + 1],
                                    None, ALU.mult).then_inc(S["sc_norm"], 1)

                for i in range(17):
                    if i < 16:
                        softmax_max(i)
                    if i:
                        softmax_norm(i - 1)

                rows_rstd(l * 3 + 3, l * 3 + 3, 96, 16, 1.0 / GW, 1e-6, 24)
                for g in range(4):
                    if g >= 2:
                        v.wait_ge(S["r_bcast"], l * 9 + 5 + g - 1)
                    diagonals(g % 2, [24 + 4 * g + b for b in range(NB)], True)
                for g in range(4):
                    v.wait_ge(S["r_bcast"], l * 9 + 5 + g + 1)
                    for c in range(2):
                        V.scalar_tensor_tensor(ym[:, 2 * g + c, :], ym[:, 2 * g + c, :], p_a("merge", 2 * g + c, 1),
                                               banks[g][:, :], ALU.mult, ALU.mult).then_inc(S["y_out"], 1)
                for k in range(KD):
                    v.wait_ge(S["y_hi"], l * KD + (k + 1))
                    V.tensor_tensor(ym_r[:, k, :], ym[:, k, :], yh[:, k, :].bitcast(F32), ALU.subtract)\
                        .then_inc(S["y_lo"], 1)
                for m in range(KD):
                    v.wait_ge(S["resid_mm"], (2 * l) * KD + m + 1)
                    V.scalar_tensor_tensor(xa[:, m, :], banks[m % 4][:, :], g1p[:, m:m + 1], xa[:, m, :], ALU.mult, ALU.add)\
                        .then_inc(S["resid"], 1)
                V.memset(small[:, 90:91], 0.0).then_inc(S["mixers_done"], 1)
                norm(2 * l + 2)
                v.wait_ge(S["parb_in"], 16 * l + 16)
                v.wait_ge(S["ln_x"], (2 * l + 2) * KD)
                V.tensor_scalar(ga[:, :, :], p_b("ln2_g", 0, 2 * KD).rearrange("p (a b) -> p a b", a=2), p_b("ln2_a"),
                                None, ALU.mult).then_inc(S["ln_par"], 1)

                for k in range(KD):
                    v.wait_ge(S["h_hi"], l * KD + (k + 1))
                    V.tensor_tensor(hm_r[:, k, :], hm[:, k, :], ym_r[:, k, :].bitcast(F32), ALU.subtract)\
                        .then_inc(S["h_lo"], 1)

                with v.Fori(0, NP2) as i:
                    o = PB_AT["conv_w"][0]
                    for r in range(4):
                        m = i * 4 + r
                        v.wait_ge(S["up_tap"], l * (2 * KF) + i * 4 + r + 1)
                        dst, bank = cv[:, r, :], banks[2 + r]
                        V.scalar_tensor_tensor(dst[:, 1:T], bank[:, 0:T - 1], pb[:, bass.ds(m * 3 + (o + 1), 1)],
                                               dst[:, 1:T], ALU.mult, ALU.add).then_inc(S["up_mid"], 1)
                        v.wait_ge(S["up_mid"], l * (2 * KF) + i * 4 + (r + 1))
                        V.scalar_tensor_tensor(dst[:, 2:T], bank[:, 0:T - 2], pb[:, bass.ds(m * 3 + o, 1)],
                                               dst[:, 2:T], ALU.mult, ALU.add).then_inc(S["up_conv"], 1)
                        if r % 2:
                            v.wait_ge(S["up_silu"], l * KF + i * 2 + (r // 2 + 1))
                            V.tensor_tensor(hf[:, bass.ds(i * 2 + r // 2, 1), :].rearrange("p a t -> p (a t)"),
                                            cv[:, r - 1, :], cv[:, 4 + r // 2, :], ALU.mult).then_inc(S["up_h"], 1)


                def inner_low(half, tile, need):
                    v.wait_ge(S["f_hi"], need)
                    V.tensor_tensor(hs[:, 2 + half, :], tile, hs[:, half, :].bitcast(F32), ALU.subtract).then_inc(S["f_lo"], 1)

                inner_low(0, hf[:, 0, :], l * KF + 1)
                with v.Fori(0, KF // 4) as i:
                    for r in range(4):
                        inner_low((1 + r) % 2, hf[:, bass.ds(i * 4 + (1 + r), 1), :].rearrange("p a t -> p (a t)"),
                                  l * KF + i * 4 + (r + 2))
                inner_low((KF - 1) % 2, hf[:, KF - 1, :], l * KF + KF)
                for n, m in enumerate(DOWN_DONE):
                    v.wait_ge(S["resid_mm"], (2 * l + 1) * KD + (n + 1))
                    V.scalar_tensor_tensor(xa[:, m, :], banks[m][:, :], g2p[:, m:m + 1], xa[:, m, :], ALU.mult, ALU.add)\
                        .then_inc(S["resid"], 1)
                norm(2 * l + 3)
                V.memset(small[:, 94:95], 0.0).then_inc(S["layer_done"], 1)
                ch.close(V.memset(idle_col(), 0.0))

        @block.scalar
        def _(a):
            A = nc.scalar.activation
            carry[a] = lambda: A(idle_col(), c_f("half_pi"), ACT.Identity)
            ch = Chain(a, S["act_chain"], 256)

            def norm_square(before, n, k):
                if before is not None:
                    a.wait_ge(S["resid"], before + (n + 1))
                A(hm[:, k, :], xa[:, k, :], ACT.Square).then_inc(S["ln_sq"], 1)

            def norm(n):
                a.wait_ge(S["ln_var"], n)
                A(st[:, 8:12], st[:, 8:12], ACT.Sqrt).then_inc(S["ln_sd"], 1)
                a.wait_ge(S["ln_par"], n)
                for k in range(KD):
                    a.wait_ge(S["ln_normed"], (n - 1) * KD + (k + 1))
                    A(xa[:, k, :], xa[:, k, :], ACT.Identity, scale=ga[:, 0, k:k + 1], bias=ga[:, 1, k:k + 1])\
                        .then_inc(S["ln_x"], 1)

            a.wait_ge(S["const_in"], 16)
            a.wait_ge(S["c_in"], 16)
            A(silu_c[:, :], silu_c[:, :], ACT.Silu).then_inc(S["silu_ready"], 1)
            a.wait_ge(S["x_in"], 16)
            for k in range(KD):
                norm_square(None, k, k)
            norm(1)


            def weights_high(l, q):
                n = FIRST_OUT + q
                a.wait_ge(landed[n % RING], l * (16 * SLOT_TOTAL[n % RING]) + 16 * (n // RING + 1))
                A(wh[:, n % RING, :], ring[:, n % RING, :], ACT.Identity).then_inc(S["w_hi"], 1)

            with a.Fori(0, L) as l:
                ch.layer(l)
                W = lambda i: sp_[:, i * P:(i + 1) * P]
                a.wait_ge(S["para_in"], 16 * l + 16)
                a.wait_ge(S["ada_used"], l * MOD_BODY + MOD_PRE)
                A(W(0), p_a("s5_ls"), ACT.Exp)
                A(small[:, 24:32], p_a("s5_sls"), ACT.Exp).then_inc(S["s5_ang"], 1)
                a.wait_ge(S["s5_ang"], 3 * l + 2)
                A(W(5), W(1), ACT.Exp)
                A(small[:, 32:40], small[:, 0:8], ACT.Exp)
                A(W(6), W(4), ACT.Sin, scale=-TWO_PI, bias=c_f("half_pi"))
                A(W(7), W(3), ACT.Sin, scale=-TWO_PI).then_inc(S["s5_trig"], 1)

                def turning(t):
                    a.wait_ge(S["s5_turn"], l * ST + t + 1)
                    ch.link(A(cos_t[:, t, :], sin_t[:, t, :], ACT.Abs))
                    A(sin_t[:, t, :], sin_t[:, t, :], ACT.Sin, scale=-TWO_PI)
                    A(cos_t[:, t, :], cos_t[:, t, :], ACT.Sin, scale=-TWO_PI, bias=c_f("half_pi")).then_inc(S["s5_tab"], 1)

                for j in range(NPROJ):
                    if j < ST // 2:
                        turning(2 * j)
                        turning(2 * j + 1)
                    if j == ST // 2:
                        a.wait_ge(S["s5_par"], l + 1)
                        A(small[:, 46:50], small[:, 46:50], ACT.Exp).then_inc(S["s5_ang"], 1)
                    a.wait_ge(S["proj_mm"], l * NPROJ + j + 1)
                    bank = banks[j % 2]
                    tok = bank[:, :].rearrange("p (b n) -> p b n", n=P)
                    if j in (U0, U1):
                        A(ym[:, 4 + j - U0, :], bank[:, :], ACT.Identity).then_inc(S["proj_out"], 1)
                    elif j in (F0, F1):
                        A(sg[:, j - F0, :], bank[:, :], ACT.Sigmoid).then_inc(S["proj_out"], 1)
                    elif j in (Q0, Q1):
                        A(qt[:, j - Q0, :], bank[:, :], ACT.Identity).then_inc(S["proj_out"], 1)
                    elif j in (I0, I1):
                        A(vtok[:, :, (j - I0) * P:(j - I0 + 1) * P], tok, ACT.Identity).then_inc(S["proj_out"], 1)
                    elif j in (G0, G1):
                        A(ym[:, 6 + j - G0, :], bank[:, :], ACT.Sigmoid).then_inc(S["proj_out"], 1)
                    elif j == CKV:
                        A(ckv[:, 0, :], bank[:, :], ACT.Identity).then_inc(S["proj_out"], 1)
                    elif j in (CQ0, CQ1):
                        A(cq[0:QH, j - CQ0, :], bank[0:QH, :], ACT.Identity)
                        A(kro[NOPE:QK, j - CQ0, :], bank[QH:P, :], ACT.Identity).then_inc(S["proj_out"], 1)
                    elif j in (AV0, AV1):
                        A(avt[:, :, (j - AV0) * P:(j - AV0 + 1) * P], tok, ACT.Gelu_apprx_tanh).then_inc(S["proj_out"], 1)
                    else:
                        A(ym[:, j - AU0, :], bank[:, :], ACT.Gelu_apprx_tanh).then_inc(S["proj_out"], 1)
                    if j == AV1:
                        for c in range(CT):
                            a.wait_ge(S["s5_y"], l * CT + c + 1)
                            A(ym[:, 4 + c, :], ym[:, 4 + c, :], ACT.Gelu_apprx_tanh).then_inc(S["s5_gelu"], 1)
                    if j == AV1:
                        a.wait_ge(S["hg_f"], l * CT + CT)
                        A(sg[:, 0, :], bc[:, 0, :], ACT.Ln)
                        A(sg[:, 1, :], bc[:, 1, :], ACT.Ln).then_inc(S["hg_lnf"], 1)
                    if j == AU0:
                        a.wait_ge(S["hg_arg"], l * CT + CT)
                        for c in range(CT):
                            A(ke[:, c, :], sg[:, c, :], ACT.Exp)
                        A(qe[:, 0, :], bc[:, 0, :], ACT.Exp)
                        A(qe[:, 1, :], bc[:, 1, :], ACT.Exp).then_inc(S["hg_exp"], 1)
                a.wait_ge(S["s5_glu"], l + 1)
                A(pout[:, 0, :], banks[0][:, :], ACT.Sigmoid, bias=p_a("b_glu", 0, 1))
                A(pout[:, 1, :], banks[1][:, :], ACT.Sigmoid, bias=p_a("b_glu", 1, 1)).then_inc(S["s5_gate"], 1)

                a.wait_ge(S["hg_ktr"], l + 1)
                A(ketok[:, 0, :], banks[2][:, :], ACT.Identity)
                A(ketok[:, 1, :], banks[3][:, :], ACT.Identity).then_inc(S["hg_ktok"], 1)
                for s in range(2 * len(LEVELS)):
                    a.wait_ge(S["hg_larg"], l * 12 + s + 1)
                    A(ee[:, s % 4, :], ee[:, s % 4, :], ACT.Exp).then_inc(S["hg_lexp"], 1)
                a.wait_ge(S["gm_var"], l + 1)
                A(st[:, 56:60], st[:, 56:60], ACT.Sqrt).then_inc(S["gm_sd"], 1)
                a.wait_ge(S["hg_omm"], l + 1)
                A(ke[:, 0, :], banks[4][:, :], ACT.Square)
                A(ke[:, 1, :], banks[5][:, :], ACT.Square).then_inc(S["hg_osq"], 1)
                a.wait_ge(S["r_var"], l * 3 + 1)
                A(st[:, 24:40], st[:, 24:40], ACT.Sqrt).then_inc(S["r_sd"], 1)

                a.wait_ge(S["r_stat"], l * 3 + 1)
                A(ke[0:QH, 0, :], cq[0:QH, 0, :], ACT.Square)
                A(ke[0:QH, 1, :], cq[0:QH, 1, :], ACT.Square)
                A(qe[:, 0, :], ckv[:, 0, :], ACT.Square).then_inc(S["r_sq"], 1)
                a.wait_ge(S["r_var"], l * 3 + 2)
                A(st[:, 40:48], st[:, 40:48], ACT.Sqrt).then_inc(S["r_sd"], 1)
                a.wait_ge(S["s5_done"], l * CT + CT)
                a.wait_ge(S["hg_done"], l + 1)
                a.wait_ge(S["gm_done"], l * CT + CT)
                for k in (4, 5, 6, 7, 0, 1):
                    A(hm[:, k, :], ym[:, k, :], ACT.Square).then_inc(S["m_sq"], 1)
                for h in range(HEADS):
                    a.wait_ge(S["k_mm"], l * HEADS + h + 1)
                    A(kt[0:NOPE, h, :], banks[4 + h % 2][0:NOPE, :], ACT.Identity).then_inc(S["k_out"], 1)
                for b in range(NB):
                    a.wait_ge(S["v_mm"], l * NB + b + 1)
                    A(vb[:, b, :], (banks[6] if b % 2 == 0 else banks[4])[:, 0:GW], ACT.Identity).then_inc(S["v_out"], 1)

                neg_max, row_sum = small[:, 75:78], small[:, 78:81]

                def soft_exp(i):
                    b, q = i % NB, i % 3
                    a.wait_ge(S["sc_max"], l * 16 + i + 1)
                    if i >= 3:
                        a.wait_ge(S["pt_mm"], l * 16 + i - 2)
                        a.wait_ge(S["sc_norm"], l * 16 + i - 2)
                    A(pp[:, q, 0:(b + 1) * P], sc_banks[q][:, 0:(b + 1) * P], ACT.Exp, scale=SCALE,
                      bias=neg_max[:, q:q + 1], accum_out=row_sum[:, q:q + 1]).then_inc(S["sc_exp"], 1)

                def turned(i):
                    b = i % NB
                    a.wait_ge(S["pt_mm"], l * 16 + i + 1)
                    if i >= 2:
                        a.wait_ge(S["pv_mm"], l * 16 + i - 1)
                    A(ptt[:, i % 2, 0:(b + 1) * P], banks[2 + i % 2][:, 0:(b + 1) * P], ACT.Identity).then_inc(S["pt_out"], 1)

                for i in range(18):
                    if i < 16:
                        soft_exp(i)
                    if i >= 2:
                        turned(i - 2)
                a.wait_ge(S["pv_mm"], l * 16 + 16)
                for c in range(CT):
                    A(ym[:, 2 + c, :], banks[4 + c][:, :], ACT.Identity).then_inc(S["mla_done"], 1)

                a.wait_ge(S["mla_done"], l * CT + CT)
                A(hm[:, 2, :], ym[:, 2, :], ACT.Square)
                A(hm[:, 3, :], ym[:, 3, :], ACT.Square).then_inc(S["r_sq"], 1)
                a.wait_ge(S["r_var"], l * 3 + 3)
                A(st[:, 24:40], st[:, 24:40], ACT.Sqrt).then_inc(S["r_sd"], 1)
                for q in range(AHEAD):
                    weights_high(l, q)
                for k in range(KD):
                    a.wait_ge(S["y_out"], l * KD + (k + 1))
                    A(yh[:, k, :], ym[:, k, :], ACT.Identity).then_inc(S["y_hi"], 1)
                for m in range(KD):
                    weights_high(l, AHEAD + m)
                    norm_square((2 * l) * KD, m, m)
                norm(2 * l + 2)
                for k in range(KD):
                    a.wait_ge(S["h_ready"], (2 * l + 1) * KD + (k + 1))
                    A(ym_r[:, k, :], hm[:, k, :], ACT.Identity).then_inc(S["h_hi"], 1)

                o, ob = PB_AT["conv_w"][0], PB_AT["conv_b"][0]
                with a.Fori(0, NP2) as i:
                    for r in range(4):
                        m = i * 4 + r
                        a.wait_ge(S["up_h"], l * KF + i * 2 + (r // 2 + 1))
                        wait_apart(a, S["up_mm"], l * (2 * KF) + i * 4 + r + 1)
                        A(cv[:, r, :], banks[2 + r][:, :], ACT.Identity, scale=pb[:, bass.ds(m * 3 + (o + 2), 1)],
                          bias=pb[:, bass.ds(m + ob, 1)]).then_inc(S["up_tap"], 1)
                        if r % 2:
                            a.wait_ge(S["up_conv"], l * (2 * KF) + i * 4 + r + 1 + 4)
                            A(cv[:, 4 + r // 2, :], cv[:, r, :], ACT.Silu).then_inc(S["up_silu"], 1)
                        n = FIRST_UP + AHEAD + r
                        a.wait_ge(landed[n % RING], l * (16 * SLOT_TOTAL[n % RING]) + i * 16 + 16 * (n // RING + 1))
                        A(wh[:, n % RING, :], ring[:, n % RING, :], ACT.Identity).then_inc(S["w_hi"], 1)

                def inner_high(half, tile, need):
                    if need is not None:
                        wait_apart(a, S["down_mm"], need)
                    A(hs[:, half, :], tile, ACT.Identity).then_inc(S["f_hi"], 1)

                w_down0 = FIRST_DOWN - FIRST_OUT
                wait_apart(a, S["up_h"], l * KF + (KF + 2))
                inner_high(0, hf[:, 0, :], None)
                inner_high(1, hf[:, 1, :], None)
                with a.Fori(0, KF // 4 - 1) as i:
                    for r in range(4):
                        n = FIRST_DOWN + AHEAD + r
                        inner_high(r % 2, hf[:, bass.ds(i * 4 + (2 + r), 1), :].rearrange("p a t -> p (a t)"),
                                   l * (KF - 1) + i * 4 + (r + 1))
                        a.wait_ge(landed[n % RING], l * (16 * SLOT_TOTAL[n % RING]) + i * 16 + 16 * (n // RING + 1))
                        A(wh[:, n % RING, :], ring[:, n % RING, :], ACT.Identity).then_inc(S["w_hi"], 1)
                done = KF // 4 * 4 - 4 + 2
                for k in range(done, KF):
                    inner_high(k % 2, hf[:, k, :], l * (KF - 1) + (k - 1))
                    if k - 2 + AHEAD < KF:
                        weights_high(l, w_down0 + k - 2 + AHEAD)
                for n, k in enumerate(DOWN_DONE):
                    norm_square((2 * l + 1) * KD, n, k)
                norm(2 * l + 3)
                ch.close(A(idle_col(), c_f("half_pi"), ACT.Identity))

        @block.gpsimd
        def _(g):
            G = nc.gpsimd
            carry[g] = lambda: G.tensor_tensor(idle_col(), c_f("half_pi"), c_f("half_pi"), ALU.add)
            g.wait_ge(S["const_in"], 16)
            ch = Chain(g, S["pool_chain"], 64)

            def modulate(l, which, scale, shift):
                for k in range(KD):
                    if k == 0 and which:
                        g.wait_ge(S["mod_ready"], l + 1)
                    wait_apart(g, S["ln_x"], (2 * l + which) * KD + (k + 1))
                    G.tensor_scalar(hm[:, k, :], xa[:, k, :], scale[:, k:k + 1], shift[:, k:k + 1], ALU.mult, ALU.add)\
                        .then_inc(S["h_ready"], 1)

            with g.Fori(0, L) as l:
                ch.layer(l)
                wait_apart(g, S["ada_used"], l * MOD_L + 2 * KD)
                ch.post(G.tensor_tensor(mod[:, 0:16], mods[:, bass.ds(l * MOD_L, 16)],
                                        c_f("b_ada")[:, bass.ds(l * MOD_L, 16)], ALU.add))
                ch.settle_apart()
                ch.post(G.tensor_scalar(s1c[:, :], mod[:, 8:16], 1.0, 1.0 / ALPHA, ALU.add, ALU.mult))
                ch.settle_apart()
                modulate(l, 0, s1c, mod[:, 0:8])
                wait_apart(g, S["s5_ang"], 3 * l + 2)
                for t in range(ST):
                    ch.post(G.tensor_scalar(cos_t[:, t, :], c_f("iota"), small[:, 8 + t:9 + t], 0.0, ALU.mult, ALU.add))
                    ch.settle_apart()
                    ch.post(G.tensor_scalar(sin_t[:, t, :], cos_t[:, t, :], 1.0, MAGIC, ALU.mult, ALU.add))
                    ch.settle_apart()
                    ch.link(G.tensor_scalar(sin_t[:, t, :], sin_t[:, t, :], 1.0, -MAGIC, ALU.mult, ALU.add))
                    G.tensor_tensor(sin_t[:, t, :], sin_t[:, t, :], cos_t[:, t, :], ALU.subtract).then_inc(S["s5_turn"], 1)

                def add_in(t):
                    g.wait_ge(S["s5_pin"], l * ST + (t + 1))
                    if t:
                        g.wait_ge(S["s5_pout"], l * ST + t)
                    G.tensor_tensor(bp[:, 0, :], pin[:, 0, :], pin[:, 1, :], ALU.add)
                    G.tensor_tensor(bp[:, 1, :], pin[:, 2, :], pin[:, 3, :], ALU.subtract).then_inc(S["s5_bp"], 1)

                def add_out(t):
                    g.wait_ge(S["s5_pout"], l * ST + (t + 1))
                    if t:
                        g.wait_ge(S["s5_c"], l * ST + t)
                    G.tensor_tensor(hh[:, 0, :], pout[:, 0, :], pout[:, 1, :], ALU.subtract)
                    G.tensor_tensor(hh[:, 1, :], pout[:, 2, :], pout[:, 3, :], ALU.add).then_inc(S["s5_h"], 1)

                for t in range(ST + 1):
                    if t < ST:
                        add_in(t)
                    if t:
                        add_out(t - 1)
                G.memset(att[:, :, :], 0.0)
                G.memset(sbd[:, :, :], 0.0).then_inc(S["hg_zero"], 1)

                def weights_low(n, need):
                    g.wait_ge(S["w_hi"], need)
                    G.tensor_tensor(ring_r[:, n % RING, :], ring[:, n % RING, :], wh[:, n % RING, :].bitcast(F32),
                                    ALU.subtract)\
                        .then_inc(S["w_lo"], 1)

                for q in range(KD + AHEAD):
                    weights_low(FIRST_OUT + q, l * NSPLIT + (q + 1))
                modulate(l, 1, s2c, mod[:, 24:32])
                q0 = KD + AHEAD
                with g.Fori(0, (NSPLIT - q0) // 4) as i:
                    for r in range(4):
                        weights_low(FIRST_OUT + q0 + r, l * NSPLIT + i * 4 + (q0 + r + 1))
                for q in range(q0 + (NSPLIT - q0) // 4 * 4, NSPLIT):
                    weights_low(FIRST_OUT + q, l * NSPLIT + (q + 1))
                ch.close(G.memset(idle_col(), 0.0))


def kernel(**inputs):
    import numpy as np
    import concourse.bacc as _bacc
    from concourse.bass_utils import run_bass_kernel_spmd as _run

    a = {k: np.asarray(v) for k, v in inputs.items()}

    def cols(v):
        return np.swapaxes(v.reshape(*v.shape[:-1], -1, P), -1, -2)

    def chunks(w, nk=KD):
        n = w.shape[2] // P
        return w.reshape(L, nk, P, n, P).transpose(0, 3, 2, 1, 4)

    wi = a["w_in"]
    sizes = (GW, GW, QR, P, ROPE, GW, GW, GW, GW, GW)
    at = np.cumsum((0,) + sizes)
    au, av, cq, ckv, kr, cu, dq, df, di, dg = (wi[:, :, at[i]:at[i + 1]] for i in range(10))
    krs = np.concatenate([kr[:, :, ROPE // 2:], kr[:, :, :ROPE // 2]], 2)
    win = np.concatenate([cu, df, dq, di, dg, ckv, cq[:, :, :QH], kr, cq[:, :, QH:], krs, av, au], 2)
    up = a["w_up"].reshape(L, D, 2, KF, P).transpose(0, 1, 3, 2, 4).reshape(L, D, 2 * DFF)
    pairs = lambda v: v.reshape(*v.shape[:-1], 2, KF, P).swapaxes(-3, -2).reshape(*v.shape[:-1], 2 * DFF)

    def pad(v):
        out = np.zeros((L, P, v.shape[2]), np.float32)
        out[:, :v.shape[1]] = v
        return out

    wide = lambda v: np.broadcast_to(v.reshape(L, 1, -1), (L, P, v.reshape(L, -1).shape[1]))
    chan = lambda v: np.repeat(v.reshape(L, CT, 8, -1), 16, 2).transpose(0, 2, 1, 3).reshape(L, P, -1)
    stat = lambda v: v.reshape(L, ST, P).transpose(0, 2, 1)
    uq = a["mla_w_uq"].reshape(L, 2, QH, HEADS, QK)
    rot = uq[..., NOPE:]
    uqs = np.concatenate([rot[..., ROPE // 2:], rot[..., :ROPE // 2]], -1)
    ukv = a["mla_w_ukv"].reshape(L, P, HEADS, NOPE + HD)
    ls = a["s5_log_step"]
    par = {
        "gm_g": wide(a["gm_ln_g"]), "gm_b": wide(a["gm_ln_b"]),
        "gm_ws": a["gm_ws"].transpose(0, 3, 1, 2).reshape(L, P, -1),
        "gm_bs": np.repeat(a["gm_bs"].reshape(L, CT, 2, P), HD, 2).transpose(0, 2, 1, 3).reshape(L, P, -1),
        "q_norm": pad(a["mla_q_norm"].reshape(L, 2, QH).transpose(0, 2, 1)), "kv_norm": a["mla_kv_norm"][:, :, None],
        "w_uq": pad(uq.transpose(0, 2, 1, 3, 4).reshape(L, QH, -1)),
        "w_uqs": pad(uqs.transpose(0, 2, 1, 3, 4).reshape(L, QH, -1)),
        "w_ukv": np.concatenate([ukv[..., :NOPE].reshape(L, P, -1), ukv[..., NOPE:].reshape(L, P, -1)], 2),
        "s5_are": chan(a["s5_a_re"]), "s5_aim": chan(a["s5_a_im"]),
        "s5_ls": chan(np.repeat(ls[:, :, None], 64, 2)),
        "s5_bre": a["s5_b_re"].transpose(0, 1, 3, 2).reshape(L, CT, P, 64).transpose(0, 2, 1, 3).reshape(L, P, -1),
        "s5_bim": a["s5_b_im"].transpose(0, 1, 3, 2).reshape(L, CT, P, 64).transpose(0, 2, 1, 3).reshape(L, P, -1),
        "s5_cre": a["s5_c_re"].transpose(0, 1, 3, 2).reshape(L, ST, P, 16).transpose(0, 2, 1, 3).reshape(L, P, -1),
        "s5_cim": a["s5_c_im"].transpose(0, 1, 3, 2).reshape(L, ST, P, 16).transpose(0, 2, 1, 3).reshape(L, P, -1),
        "s5_sre": stat(a["s5_a_re"]), "s5_sim": stat(a["s5_a_im"]), "s5_sls": stat(np.repeat(ls[:, :, None], 64, 2)),
        "s5_d": cols(a["s5_d"]), "w_glu": a["s5_w_glu"].reshape(L, CT, P, GW).transpose(0, 2, 1, 3).reshape(L, P, -1),
        "b_glu": cols(a["s5_b_glu"]),
        "hg_lb": np.broadcast_to(a["hg_lb_logits"].reshape(1, L, CT, P).transpose(0, 3, 2, 1), (L, P, CT, L)).reshape(L, P, -1),
        "hg_sel": np.broadcast_to(np.array([[1.0 if 1 <= j <= l else 0.0 for j in range(L)] for l in range(L)],
                                           np.float32).reshape(L, 1, 1, L), (L, P, CT, L)).reshape(L, P, -1),
        "hg_g": cols(a["hg_norm_g"]), "merge": cols(a["merge_g"]), "ln1_g": cols(a["ln1_g"]), "ln1_b": cols(a["ln1_b"]),
        "conv_w": cols(pairs(a["conv_w"])).transpose(0, 2, 3, 1).reshape(L, P, -1), "conv_b": cols(pairs(a["conv_b"])),
        "ln2_g": cols(a["ln2_g"]), "ln2_b": cols(a["ln2_b"]),
        "ln2_a": np.array([ALPHA] * (L - 1) + [1.0], np.float32).reshape(L, 1, 1) + np.zeros((1, P, 1), np.float32),
    }
    pack = lambda names: np.concatenate([par[n].reshape(L, P, w) for n, w in names], 2)

    p = np.arange(P)
    t = np.arange(T)
    inv = np.float32(1.0) / (np.float32(10000.0) ** (np.arange(0, ROPE, 2, dtype=np.float32) / np.float32(ROPE)))
    ang = (t.astype(np.float32)[None, :] * inv[:, None]).astype(np.float64)
    rc, rs = np.ones((P, T)), np.zeros((P, T))
    rc[NOPE:QK] = np.concatenate([np.cos(ang), np.cos(ang)])
    rs[NOPE:QK] = np.concatenate([-np.sin(ang), np.sin(ang)])
    head = np.stack([p // 64 == g for g in range(2)], 1).astype(float)
    const = {
        "rope_c": rc, "rope_s": rs, "iota": np.tile(t, (P, 1)), "reset": np.tile(t % CHUNK != 0, (P, 1)),
        "ident": np.eye(P), "ones": np.ones((P, P)), "head": head, "nhead": 0.0 - head,
        "pair": np.stack([(p // 16) % 2 == g for g in range(2)], 1), "half_pi": np.full((P, 1), 1.5707963),
        "mask_q": np.tile(p < CHUNK, (P, 1)), "mask_k": np.tile(np.where(p >= CHUNK, NEG, 0.0), (P, 1)),
    }
    s_, t_ = p[:, None], p[None, :]
    const["levels"] = np.stack([(s_ // (2 * w) == t_ // (2 * w)) & (s_ % (2 * w) < w) & (t_ % (2 * w) >= w)
                                for w in LEVELS] + [s_ == t_], 1)
    const = {k: v.astype(np.float32) for k, v in const.items()}
    const.update(b_ada=cols(a["b_ada"].reshape(-1)), lng=cols(a["ln_in_g"]), lnb=cols(a["ln_in_b"]))
    consts = np.concatenate([const[n].reshape(P, w) for n, w in CF], 1)

    arrays = {
        "x": np.swapaxes(a["x"][0].T.reshape(KD, P, T), 0, 1), "consts": consts,
        "c_row": np.broadcast_to(a["c"], (P, D)), "par_a": pack(PA), "par_b": pack(PB),
        "w_ada": a["w_ada"].swapaxes(1, 2).reshape(L + 1, MOD_BODY, P, D), "w_in": chunks(win),
        "w_out": chunks(a["w_out"]), "w_up": chunks(up), "w_down": a["w_down"].reshape(L, KF, P, D),
    }
    nc = _bacc.Bacc("TRN2", target_bir_lowering=False, num_devices=1)
    args = []
    for n, v in arrays.items():
        v = np.ascontiguousarray(v)
        if v.ndim == 5:
            v = v.reshape(*v.shape[:3], -1)
        arrays[n] = v
        args.append(nc.dram_tensor(f"in_{n}", v.shape, mybir.dt.from_np(v.dtype), kind="ExternalInput").ap())
    args.append(nc.dram_tensor("out_0", (P, KD, T), F32, kind="ExternalOutput").ap())
    trunk(nc, *args)
    r = _run(nc, [{f"in_{n}": v for n, v in arrays.items()}], core_ids=[0])
    got = r.results[0]["out_0"]
    return np.swapaxes(got, 0, 1).reshape(1, D, T).swapaxes(1, 2)
```
